# Optimizing a Trainium2 kernel written in Bass

```python
import jax, jax.numpy as jnp
from jax import lax
import numpy as np

D_MODEL = 1024
BATCH = 1
SEQ = 128
DEPTH = 1
DEC_BATCH = 1
DEC_SEQ = 512
PAST_LEN = 128

GRID_W = 64
N_FOURIER_GROUPS = 4
FOURIER_GROUP_DIM = 128
D_FOURIER = N_FOURIER_GROUPS * FOURIER_GROUP_DIM
RWKV_HEAD_DIM = 64
D_RWKV = D_MODEL
N_RWKV_HEADS = D_RWKV // RWKV_HEAD_DIM
LORA_W = 64
LORA_A = 64
LORA_G = 128
N_DIR = 2
SHORT_CONV = 3
GN_EPS = 64e-5
N_EXPERTS = 16
CAPACITY_FACTOR = 2
D_EXPERT = 2048
LN_EPS = 1e-5
DEEPNORM_ALPHA = (2.0 * DEPTH) ** 0.25
DEEPNORM_BETA = (8.0 * DEPTH) ** -0.25
IN_WIDTHS = (D_FOURIER, 3 * D_RWKV, N_DIR * LORA_W, N_DIR * LORA_A, LORA_G, D_MODEL, D_MODEL)
D_IN = sum(IN_WIDTHS)
SPLIT_POINTS = tuple(sum(IN_WIDTHS[:i + 1]) for i in range(len(IN_WIDTHS) - 1))

kernel_name = "fnet_rwkv7_ec_moe_diffusion_step"

def layer_norm(x, g, b):
    xf = x.astype(jnp.float32)
    mu = jnp.mean(xf, axis=-1, keepdims=True)
    var = jnp.mean(jnp.square(xf - mu), axis=-1, keepdims=True)
    return ((xf - mu) * lax.rsqrt(var + LN_EPS) * g + b).astype(x.dtype)

def to_heads(t):
    return t.reshape(*t.shape[:-1], N_RWKV_HEADS, RWKV_HEAD_DIM)

def centred_conv(u, w):
    t = u.shape[1]
    pad = SHORT_CONV // 2
    up = jnp.pad(u, ((0, 0), (pad, pad), (0, 0)))
    out = up[:, 0:t] * w[0]
    for i in range(1, SHORT_CONV):
        out = out + up[:, i:i + t] * w[i]
    return out

def fourier_mix(u):
    b, t, _ = u.shape
    ug = u.astype(jnp.float32).reshape(b, t, N_FOURIER_GROUPS, FOURIER_GROUP_DIM)
    f = jnp.fft.fft2(ug, axes=(1, 3), norm="ortho").real
    return f.reshape(b, t, D_FOURIER).astype(u.dtype)

def wkv7_scan(r, w, k, v, kk, a, s0, reverse):
    def step(S, inp):
        r_t, w_t, k_t, v_t, kk_t, a_t = inp
        sa = jnp.einsum('bhij,bhj->bhi', S, -kk_t)
        S = (S * w_t[:, :, None, :] + sa[..., None] * (kk_t * a_t)[:, :, None, :]
             + v_t[..., None] * k_t[:, :, None, :])
        y = jnp.einsum('bhij,bhj->bhi', S, r_t)
        return S, y
    xs = tuple(jnp.swapaxes(t, 0, 1) for t in (r, w, k, v, kk, a))
    s_final, ys = lax.scan(step, s0, xs, reverse=reverse)
    return jnp.swapaxes(ys, 0, 1), s_final

def rwkv7_direction(r, k, v, kk, decay, a_rate, k_a, r_k, s0, reverse):
    k_d = to_heads(k * (1.0 + (a_rate - 1.0) * k_a))
    y, s_final = wkv7_scan(r, to_heads(decay), k_d, v, kk, to_heads(a_rate),
                           s0.astype(jnp.float32), reverse)
    bonus = jnp.sum(r * k_d * r_k, axis=-1, keepdims=True) * v
    return y, bonus, s_final

def parallel_mixer(h, s_f0, s_b0, w_in, conv_w, w_decay0, w_decay_up, a0, a_up, g_up,
                   k_k, k_a, r_k, gn_g, gn_b, w_fo, w_ro, w_out):
    b, t, _ = h.shape
    proj = h @ w_in
    u_f, rkv, w_dn, a_dn, g_dn, gate_f, gate_r = jnp.split(proj, SPLIT_POINTS, axis=-1)
    o_f = fourier_mix(u_f) @ w_fo
    rkv = centred_conv(rkv, conv_w).astype(jnp.float32)
    r, k, v = jnp.split(rkv, 3, axis=-1)
    w_dn = w_dn.reshape(b, t, N_DIR, LORA_W).astype(jnp.float32)
    a_dn = a_dn.reshape(b, t, N_DIR, LORA_A).astype(jnp.float32)
    w_log = -jax.nn.softplus(-(w_decay0 + jnp.einsum('btdr,drc->btdc', jnp.tanh(w_dn), w_decay_up))) - 0.5
    decay = jnp.exp(-jnp.exp(w_log))
    a_rate = jax.nn.sigmoid(a0 + jnp.einsum('btdr,drc->btdc', a_dn, a_up))
    g = jax.nn.sigmoid(g_dn) @ g_up
    kk = to_heads(k * k_k)
    kk = kk * lax.rsqrt(jnp.sum(jnp.square(kk), axis=-1, keepdims=True) + 1e-12)
    r_h, v_h = to_heads(r), to_heads(v)
    y_f, bonus_f, s_f = rwkv7_direction(r_h, k, v_h, kk, decay[:, :, 0], a_rate[:, :, 0], k_a, r_k, s_f0, False)
    y_b, bonus_b, s_b = rwkv7_direction(r_h, k, v_h, kk, decay[:, :, 1], a_rate[:, :, 1], k_a, r_k, s_b0, True)
    y = y_f + y_b
    mu = jnp.mean(y, axis=-1, keepdims=True)
    var = jnp.mean(jnp.square(y - mu), axis=-1, keepdims=True)
    y = ((y - mu) * lax.rsqrt(var + GN_EPS)).reshape(b, t, D_RWKV) * gn_g + gn_b
    y = y + (bonus_f + bonus_b).reshape(b, t, D_RWKV)
    o_r = (y * g).astype(h.dtype) @ w_ro
    merged = jax.nn.sigmoid(gate_f) * o_f + jax.nn.sigmoid(gate_r) * o_r
    return merged @ w_out, s_f, s_b

def expert_choice_ffn(h, w_router, w_e1, w_e3, w_e2):
    b, t, d = h.shape
    n = b * t
    cap = CAPACITY_FACTOR * n // N_EXPERTS
    hf = h.reshape(n, d)
    aff = jax.nn.softmax((hf @ w_router).astype(jnp.float32), axis=-1)
    gate, idx = lax.top_k(aff.T, cap)
    xe = hf[idx]
    he = jax.nn.silu(jnp.einsum('ecd,edf->ecf', xe, w_e1)) * jnp.einsum('ecd,edf->ecf', xe, w_e3)
    ye = jnp.einsum('ecf,efd->ecd', he, w_e2) * gate[..., None].astype(h.dtype)
    out = jnp.zeros_like(hf).at[idx.reshape(-1)].add(ye.reshape(-1, d))
    return out.reshape(b, t, d)

def trunk_layer(x, cond, s_f0, s_b0, w_ada, b_ada, w_in, conv_w, w_decay0, w_decay_up, a0, a_up,
                g_up, k_k, k_a, r_k, gn_g, gn_b, w_fo, w_ro, w_out, ln1_g, ln1_b,
                w_router, w_e1, w_e3, w_e2, ln2_g, ln2_b):
    mod = (jax.nn.silu(cond) @ w_ada + b_ada)[:, None, :]
    sh1, sc1, g1, sh2, sc2, g2 = jnp.split(mod, 6, axis=-1)
    h = x * (1.0 + sc1) + sh1
    mix, s_f, s_b = parallel_mixer(h, s_f0, s_b0, w_in, conv_w, w_decay0, w_decay_up, a0, a_up, g_up,
                                   k_k, k_a, r_k, gn_g, gn_b, w_fo, w_ro, w_out)
    x = layer_norm(DEEPNORM_ALPHA * x + g1 * mix, ln1_g, ln1_b)
    h2 = x * (1.0 + sc2) + sh2
    x = layer_norm(DEEPNORM_ALPHA * x + g2 * expert_choice_ffn(h2, w_router, w_e1, w_e3, w_e2), ln2_g, ln2_b)
    return x, s_f, s_b

def setup_inputs(seed: int = 0) -> dict:
    key = jax.random.key(seed)
    ks = iter(jax.random.split(key, 40))
    nrm = lambda shape, s: jax.random.normal(next(ks), shape, jnp.float32) * s
    D, R, H, N, E, L = D_MODEL, D_RWKV, N_RWKV_HEADS, RWKV_HEAD_DIM, N_EXPERTS, DEPTH
    conv_center = jnp.zeros((SHORT_CONV, 1), jnp.float32).at[SHORT_CONV // 2].set(1.0)
    return {
        "x_prompt": nrm((BATCH, SEQ, D), 1.0),
        "x_sample": nrm((DEC_BATCH, DEC_SEQ, D), 1.0),
        "state_fwd": nrm((DEC_BATCH, L, H, N, N), 0.5),
        "state_bwd": nrm((DEC_BATCH, L, H, N, N), 0.5),
        "c": nrm((DEC_BATCH, D), 1.0),
        "c_ctx": nrm((D,), 1.0),
        "w_ada": nrm((L, D, 6 * D), 0.5 * D ** -0.5),
        "b_ada": nrm((L, 6 * D), 0.02),
        "w_in": nrm((L, D, D_IN), D ** -0.5),
        "conv_w": conv_center + nrm((L, SHORT_CONV, 3 * R), 0.2),
        "w_decay0": jax.random.uniform(next(ks), (L, N_DIR, R), jnp.float32, -6.0, -1.0),
        "w_decay_up": nrm((L, N_DIR, LORA_W, R), 0.1 * LORA_W ** -0.5),
        "a0": nrm((L, N_DIR, R), 0.1),
        "a_up": nrm((L, N_DIR, LORA_A, R), 0.1 * LORA_A ** -0.5),
        "g_up": nrm((L, LORA_G, R), LORA_G ** -0.5),
        "k_k": 0.85 + nrm((L, R), 0.05),
        "k_a": 1.0 + nrm((L, R), 0.05),
        "r_k": nrm((L, H, N), 0.1),
        "gn_g": 1.0 + nrm((L, R), 0.05),
        "gn_b": nrm((L, R), 0.02),
        "w_fo": nrm((L, D_FOURIER, D), D_FOURIER ** -0.5),
        "w_ro": nrm((L, R, D), R ** -0.5),
        "w_out": nrm((L, D, D), DEEPNORM_BETA * D ** -0.5),
        "ln1_g": 1.0 + nrm((L, D), 0.05),
        "ln1_b": nrm((L, D), 0.02),
        "w_router": nrm((L, D, E), D ** -0.5),
        "w_e1": nrm((L, E, D, D_EXPERT), D ** -0.5),
        "w_e3": nrm((L, E, D, D_EXPERT), D ** -0.5),
        "w_e2": nrm((L, E, D_EXPERT, D), DEEPNORM_BETA * D_EXPERT ** -0.5),
        "ln2_g": 1.0 + nrm((L, D), 0.05),
        "ln2_b": nrm((L, D), 0.02),
    }

def reference(x_prompt, x_sample, state_fwd, state_bwd, c, c_ctx, w_ada, b_ada, w_in, conv_w,
              w_decay0, w_decay_up, a0, a_up, g_up, k_k, k_a, r_k, gn_g, gn_b, w_fo, w_ro, w_out,
              ln1_g, ln1_b, w_router, w_e1, w_e3, w_e2, ln2_g, ln2_b):
    n_ctx_req = x_prompt.shape[0]
    cond_ctx = jnp.broadcast_to(c_ctx, (n_ctx_req, D_MODEL))
    zero_state = jnp.zeros((n_ctx_req, N_RWKV_HEADS, RWKV_HEAD_DIM, RWKV_HEAD_DIM), jnp.float32)
    xp, xs = x_prompt, x_sample
    new_f, new_b = [], []
    for l in range(DEPTH):
        lp = (w_ada[l], b_ada[l], w_in[l], conv_w[l], w_decay0[l], w_decay_up[l], a0[l], a_up[l],
              g_up[l], k_k[l], k_a[l], r_k[l], gn_g[l], gn_b[l], w_fo[l], w_ro[l], w_out[l],
              ln1_g[l], ln1_b[l], w_router[l], w_e1[l], w_e3[l], w_e2[l], ln2_g[l], ln2_b[l])
        xp, s_f, s_b = trunk_layer(xp, cond_ctx, zero_state, zero_state, *lp)
        new_f.append(s_f)
        new_b.append(s_b)
        xs, _, _ = trunk_layer(xs, c, state_fwd[:, l], state_bwd[:, l], *lp)
    new_state_fwd = jnp.stack(new_f, axis=1).astype(x_prompt.dtype)
    new_state_bwd = jnp.stack(new_b, axis=1).astype(x_prompt.dtype)
    return (xp, xs, new_state_fwd, new_state_bwd)


_drawn_inputs = setup_inputs


def setup_inputs(seed=0):
    import zlib

    import numpy as np

    out = dict(_drawn_inputs(seed))
    spreads = {}
    factors = {'state_fwd': 8.0,
     'state_bwd': 8.0,
     'w_decay_up': 7.616,
     'gn_g': 27.6,
     'gn_b': 64.0,
     'ln1_b': 2.833,
     'ln2_b': 2.772}
    for name, (base, spread) in spreads.items():
        noise = np.random.default_rng([zlib.crc32(name.encode()), seed]).standard_normal(out[name].shape)
        drawn = base * np.exp(spread * noise) if base else spread * noise
        out[name] = __import__('jax').numpy.asarray(drawn.astype(out[name].dtype))
    for name, factor in factors.items():
        out[name] = (out[name] * factor).astype(out[name].dtype)
    return out
```

```python
from contextlib import ExitStack

import numpy as np

import concourse.bass as bass
from concourse import mybir

F32, F32R, BF16 = mybir.dt.float32, mybir.dt.float32r, mybir.dt.bfloat16
ALU = mybir.AluOpType
ACT = mybir.ActivationFunctionType

P = 128
DM = 1024
KD = DM // P
LAT, CTX = 512, 128
TOK = LAT + CTX
NT = TOK // P
CT = NT - 1
HD = 64
FG = 4
D_IN = 6016
COL_RKV, COL_LORA, COL_GATE = 512, 3584, 3968
NE = 16
DE = 2048
CAP_L, CAP_C = 2 * LAT // NE, 2 * CTX // NE
CAP = CAP_L + CAP_C
FQ = 4
FW = DE // FQ
LEVELS = 7
DECAY = float(np.exp(-0.5))
ALPHA = float(2.0 ** 0.25)
LN_EPS, GN_EPS, KK_EPS = 1e-5, 64e-5, 1e-12
LORA = 64

(C_CONV0, C_CONV1, C_CONV2, C_DEC0, C_RATE0, C_KK, C_KA, C_RK, C_GNG, C_GNB) = (0, 3, 6, 9, 11, 13, 14, 15, 16, 17)
NPAR = 18


def shape_constants():
    c = {}
    c["ident"] = np.eye(P, dtype=np.float32)
    half = np.arange(P) // HD
    c["headones"] = (half[:, None] == half[None, :]).astype(np.float32)
    s, t = np.arange(P)[:, None], np.arange(P)[None, :]
    c["causal"] = np.stack([np.stack([s < t, s <= t], 1), np.stack([s > t, s >= t], 1)], 1).astype(np.float32)
    lev = np.zeros((P, 2, LEVELS, P), np.float32)
    for n in range(LEVELS):
        b = 1 << n
        m = (s // (2 * b) == t // (2 * b)) & ((s // b) % 2 == 1) & ((t // b) % 2 == 0)
        lev[:, 0, n], lev[:, 1, n] = m, m.T
    c["levels"] = lev
    reset = np.ones((P, TOK), np.float32)
    reset[:, ::P] = 0.0
    c["reset"] = reset

    def dft(n):
        a = 2.0 * np.pi * ((np.arange(n)[:, None] * np.arange(n)[None, :]) % n) / n
        return np.cos(a) / np.sqrt(n), np.sin(a) / np.sqrt(n)
    cc, sc = dft(P)
    c["dft_ch"] = np.concatenate([cc, sc], 1).astype(np.float32)
    cl, sl = dft(LAT)
    c["dft_lat"] = np.stack([cl, -sl]).astype(np.float32)
    cx, sx = dft(CTX)
    c["dft_ctx"] = np.concatenate([cx, -sx], 1).astype(np.float32)
    c["iota_slot"] = np.tile(np.arange(1, CAP + 1, dtype=np.float32), (P, 1))
    c["iota_tok"] = np.tile(np.arange(TOK, dtype=np.float32), (P, 1))
    c["tok_id"] = (np.arange(P)[:, None] + P * np.arange(NT)[None, :]).astype(np.float32)
    return c


def modulation_phase(nc, d, ident, x):
    CW, NCH = 512, 6 * DM // 512
    with ExitStack() as ctx:
        sb = lambda n, s: ctx.enter_context(nc.sbuf_tensor(n, s, F32))
        sem = lambda n: ctx.enter_context(nc.semaphore(n))
        cond, sig, act_c = sb("cond", [2, DM]), sb("cond_sig", [2, DM]), sb("cond_act", [2, DM])
        cT = sb("condT", [P, KD, 2])
        w = [sb(f"w_ada{j}", [P, KD, CW]) for j in range(2)]
        bias, mod = sb("b_ada_sb", [2, 6 * DM]), sb("mod_sb", [2, 6 * DM])
        psT = ctx.enter_context(nc.psum_tensor("ps_condT", [P, 512], F32))
        ps = [ctx.enter_context(nc.psum_tensor(f"ps_mod{j}", [P, 512], F32)) for j in range(2)]
        s_cond, s_bias, s_sig, s_act = sem("s_cond"), sem("s_bias"), sem("s_cond_sig"), sem("s_cond_act")
        s_tr, s_ct = sem("s_cond_tr"), sem("s_condT")
        s_w, s_mm, s_mod, s_out = [sem("s_wada0"), sem("s_wada1")], sem("s_mod_mm"), sem("s_mod_sb"), sem("s_mod_out")
        s_id, s_x, s_free = sem("s_ident"), sem("s_x"), [sem("s_mod_free0"), sem("s_mod_free1")]
        block = ctx.enter_context(nc.Block())
        w_view = d["w_ada"][0].rearrange("(k p) n -> p k n", p=P)

        @block.sync
        def _(sp):
            sp.dma_start(cond[0:1, :], d["c"]).then_inc(s_cond, 16)
            sp.dma_start(cond[1:2, :], d["c_ctx"].rearrange("(a n) -> a n", a=1)).then_inc(s_cond, 16)
            sp.dma_start(ident[:, :], d["ident"]).then_inc(s_id, 16)
            sp.dma_start(bias[0:1, :], d["b_ada"]).then_inc(s_bias, 16)
            sp.dma_start(bias[1:2, :], d["b_ada"]).then_inc(s_bias, 16)
            for j in range(2):
                sp.dma_start(w[j][:, :, :], w_view[:, :, j * CW:(j + 1) * CW]).then_inc(s_w[j], 16)
            with sp.Fori(1, NCH // 2) as i:
                for j in range(2):
                    sp.wait_ge(s_mm, 2 * i + j - 1)
                    sp.dma_start(w[j][:, :, :], w_view[:, :, bass.ts(2 * i + j, CW)]).then_inc(s_w[j], 16)
            for t in range(NT):
                src = d["x_sample"][0, t * P:(t + 1) * P, :] if t < CT else d["x_prompt"][0]
                sp.dma_start(x[:, t, :], src).then_inc(s_x, 16)
            sp.wait_ge(s_mod, 1)
            sp.dma_start(d["mod"], mod[:, :]).then_inc(s_out, 16)
            sp.wait_ge(s_out, 16)
            sp.wait_ge(s_x, 16 * NT)

        @block.scalar
        def _(act):
            act.wait_ge(s_cond, 32)
            act.activation(sig[:, :], cond[:, :], ACT.Sigmoid).then_inc(s_sig, 1)

        @block.tensor
        def _(pe):
            pe.wait_ge(s_id, 16)
            pe.wait_ge(s_act, 1)
            for k in range(KD):
                last = pe.transpose(psT[:, 2 * k:2 * k + 2], act_c[:, k * P:(k + 1) * P], ident[0:2, 0:2])
            last.then_inc(s_tr, 1)
            pe.wait_ge(s_ct, 1)

            with pe.Fori(0, NCH // 2) as i:
                for j in range(2):
                    pe.wait_ge(s_w[j], 16 * i + 16)
                    pe.wait_ge(s_free[j], i + 1)
                    for k in range(KD):
                        last = pe.matmul(ps[j][0:2, :], cT[:, k, :], w[j][:, k, :], start=(k == 0), stop=(k == KD - 1))
                    last.then_inc(s_mm, 1)

        @block.vector
        def _(v):
            v.wait_ge(s_sig, 1)
            v.tensor_tensor(act_c[:, :], cond[:, :], sig[:, :], ALU.mult).then_inc(s_act, 1)
            v.wait_ge(s_tr, 1)
            v.tensor_copy(cT[:, :, :], psT[:, 0:2 * KD].rearrange("p (k c) -> p k c", c=2)).then_inc(s_ct, 1)
            v.wait_ge(s_bias, 32)
            for j in range(2):
                v.sem_inc(s_free[j], 1)
            with v.Fori(0, NCH // 2) as i:
                for j in range(2):
                    v.wait_ge(s_mm, 2 * i + j + 1)
                    v.tensor_tensor(mod[:, bass.ts(2 * i + j, CW)], ps[j][0:2, :],
                                    bias[:, bass.ts(2 * i + j, CW)], ALU.add).then_inc(s_free[j], 1)
            v.drain().then_inc(s_mod, 1)


def input_phase(nc, d, ident, x, hT, lora):
    SH, SC = 0, DM
    NL = 3 * P
    with ExitStack() as ctx:
        sb = lambda n, s: ctx.enter_context(nc.sbuf_tensor(n, s, F32))
        sem = lambda n: ctx.enter_context(nc.semaphore(n))
        scale = [sb(f"scale1_{j}", [P, DM]) for j in range(2)]
        shift = [sb(f"shift1_{j}", [P, DM]) for j in range(2)]
        w_f, w_l = sb("w_in_fourier", [P, KD, FG * P]), sb("w_in_lora", [P, KD, NL])
        uT, fT = sb("uT", [P, FG, TOK]), sb("fourierT_out", [P, FG, TOK])
        dch, dlat, dctx = sb("dft_ch_sb", [P, 2 * P]), sb("dft_lat_sb", [P, 2, CT, LAT]), sb("dft_ctx_sb", [P, 2 * P])
        z = sb("dft_half", [P, 2, NT, 2 * P])
        wide = [ctx.enter_context(nc.psum_tensor(f"ps_in{j}", [P, 1024], F32)) for j in range(4)]
        s_mod1, s_w, s_dft = sem("s_mod1"), sem("s_w_first"), sem("s_dft")
        s_sc, s_h, s_tr, s_ht = sem("s_scale"), sem("s_h_tok"), sem("s_h_tr"), sem("s_hT")
        s_pr, s_prs = sem("s_first_mm"), sem("s_first_sb")
        s_z, s_zs, s_f, s_fs, s_fo = sem("s_dft1_mm"), sem("s_dft1_sb"), sem("s_dft2_mm"), sem("s_dft2_sb"), sem("s_dft_out")
        block = ctx.enter_context(nc.Block())

        @block.sync
        def _(sp):
            for j in range(2):
                sp.dma_start(scale[j][:, :], d["mod"][j:j + 1, SC:SC + DM].to_broadcast([P, DM])).then_inc(s_mod1, 16)
                sp.dma_start(shift[j][:, :], d["mod"][j:j + 1, SH:SH + DM].to_broadcast([P, DM])).then_inc(s_mod1, 16)
            w = d["w_in"][0].rearrange("(k p) n -> p k n", p=P)
            sp.dma_start(w_f[:, :, :], w[:, :, 0:FG * P]).then_inc(s_w, 16)
            sp.dma_start(w_l[:, :, :], w[:, :, COL_LORA:COL_LORA + NL]).then_inc(s_w, 16)
            sp.dma_start(dch[:, :], d["dft_ch"]).then_inc(s_dft, 16)
            sp.dma_start(dctx[:, :], d["dft_ctx"]).then_inc(s_dft, 16)
            for m in range(2):
                sp.dma_start(dlat[:, m, :, :], d["dft_lat"][m].rearrange("(a p) n -> p a n", p=P)).then_inc(s_dft, 16)
            for g in range(FG):
                sp.wait_ge(s_fs, g + 1)
                sp.dma_start(d["fT"][:, g, :], fT[:, g, :]).then_inc(s_fo, 16)
            sp.wait_ge(s_fo, 16 * FG)

        @block.vector
        def _(v):
            v.wait_ge(s_mod1, 64)
            for j in range(2):
                v.tensor_scalar(scale[j][:, :], scale[j][:, :], 1.0, None, ALU.add).then_inc(s_sc, 1)
            v.wait_ge(s_sc, 2)
            for t in range(NT):
                v.tensor_tensor(x[:, t, :], x[:, t, :], scale[t // CT][:, :], ALU.mult)
            v.drain()
            for t in range(NT):
                v.tensor_tensor(x[:, t, :], x[:, t, :], shift[t // CT][:, :], ALU.add)
            v.drain().then_inc(s_h, 1)
            for k in range(KD):
                v.wait_ge(s_tr, k + 1)
                v.tensor_copy(hT[:, k, :], wide[k % 4][:, 0:TOK]).then_inc(s_ht, 1)
            for g in range(FG):
                v.wait_ge(s_pr, g + 1)
                v.tensor_copy(uT[:, g, :], wide[g % 4][:, 0:TOK]).then_inc(s_prs, 1)
            for g in range(FG):
                v.wait_ge(s_f, g + 1)
                v.tensor_copy(fT[:, g, :], wide[2 + g % 2][:, 0:TOK]).then_inc(s_fs, 1)

        @block.tensor
        def _(pe):
            pe.wait_ge(s_h, 1)
            for k in range(KD):
                if k >= 4:
                    pe.wait_ge(s_ht, k - 3)
                for t in range(NT):
                    last = pe.transpose(wide[k % 4][:, t * P:(t + 1) * P], x[:, t, k * P:(k + 1) * P], ident[:, :])
                last.then_inc(s_tr, 1)
            pe.wait_ge(s_ht, KD)
            pe.wait_ge(s_w, 32)
            for n in range(FG + 3):
                if n >= 4:
                    pe.wait_ge(s_prs, n - 3)
                w = w_f[:, :, n * P:(n + 1) * P] if n < FG else w_l[:, :, (n - FG) * P:(n - FG + 1) * P]
                for c0, c1 in ((0, LAT), (LAT, TOK)):
                    for k in range(KD):
                        last = pe.matmul(wide[n % 4][:, c0:c1], w[:, k, :], hT[:, k, c0:c1], start=(k == 0), stop=(k == KD - 1))
                last.then_inc(s_pr, 1)
            pe.wait_ge(s_dft, 64)
            pe.wait_ge(s_prs, FG + 3)
            for g in range(FG):
                if g >= 1:
                    pe.wait_ge(s_zs, g)
                for t in range(NT):
                    last = pe.matmul(wide[t // 4][:, (t % 4) * 2 * P:(t % 4 + 1) * 2 * P], uT[:, g, t * P:(t + 1) * P],
                                     dch[:, :], start=True, stop=True)
                last.then_inc(s_z, 1)
                pe.wait_ge(s_zs, g + 1)
                if g >= 2:
                    pe.wait_ge(s_fs, g - 1)
                out = wide[2 + g % 2]
                for t in range(CT):
                    for m in range(2):
                        pe.matmul(out[:, 0:LAT], z[:, g % 2, t, m * P:(m + 1) * P], dlat[:, m, t, :],
                                  start=(t + m == 0), stop=(t == CT - 1 and m == 1))
                for m in range(2):
                    last = pe.matmul(out[:, LAT:TOK], z[:, g % 2, CT, m * P:(m + 1) * P], dctx[:, m * P:(m + 1) * P],
                                     start=(m == 0), stop=(m == 1))
                last.then_inc(s_f, 1)

        @block.scalar
        def _(act):
            for n, f in enumerate((ACT.Tanh, ACT.Copy, ACT.Sigmoid)):
                act.wait_ge(s_pr, FG + n + 1)
                act.wait_ge(s_prs, FG + n)
                act.activation(lora[n][:, :], wide[(FG + n) % 4][:, 0:TOK], f).then_inc(s_prs, 1)
            for g in range(FG):
                act.wait_ge(s_z, g + 1)
                if g >= 2:
                    act.wait_ge(s_f, g - 1)
                act.activation(z[:, g % 2, 0:CT, :], wide[0][:, :].rearrange("p (t n) -> p t n", t=CT), ACT.Copy)
                act.activation(z[:, g % 2, CT, :], wide[1][:, 0:2 * P], ACT.Copy)
                act.drain().then_inc(s_zs, 1)


def scan_phase(nc, d, ident, hT, lora, spare):
    NG, NPROB = NT, 4
    ORDER = [0, 3, 1, 2, 4]
    PAIRS = ((0, 3), (1, 2), (4,))
    SLOT = {0: 0, 3: 1, 1: 0, 2: 1, 4: 0}
    POS = {g: n for n, g in enumerate(ORDER)}
    rounds = [(gs, l) for gs in PAIRS for l in range(1, LEVELS)]
    ROUNDS = len(rounds)
    steps = [(g, l) for gs, l in rounds for g in gs]
    NS = len(steps)
    ND = sum(l < LEVELS - 1 for _, l in steps)
    dcount = np.cumsum([l < LEVELS - 1 for _, l in steps]).tolist()
    slot_before = {n: max([m for m in range(n) if SLOT[steps[m][0]] == SLOT[steps[n][0]]], default=None) for n in range(NS)}
    first_step = [sum(len(gs) for gs, _ in rounds[:r]) for r in range(ROUNDS)]
    (J_R, J_K, J_V, J_DEC0, J_NORM, J_DEC1, J_RATE0, J_RATE1, J_VT, J_ST, J_KT0, J_BT0, J_NONE0, J_NONE1, J_KT1, J_BT1,
     J_BONUS) = range(17)
    JOBS = [n for n in range(17) if n not in (J_NONE0, J_NONE1)]
    NJ = len(JOBS)
    CH0 = 2 * (LEVELS - 1)
    parts = [(n // 3, "XUS"[n % 3]) for n in range(3 * CT - 1)]
    latent = lambda dr, n: n if dr == 0 else CT - 1 - n

    with ExitStack() as ctx:
        sb = lambda n, s, dt=F32: ctx.enter_context(nc.sbuf_tensor(n, s, dt))
        sem = lambda n: ctx.enter_context(nc.semaphore(n))
        par, cur = sb("par", [P, NPAR, KD]), [sb(f"par_cur{n}", [P, NPAR]) for n in range(2)]
        headones, headmean = sb("headones_sb", [P, P]), sb("headmean_sb", [P, P])
        causal, levels = sb("causal_sb", [P, 2, 2, P], BF16), sb("levels_sb", [P, 2, LEVELS, P], BF16)
        reset = sb("reset_sb", [P, TOK])
        w_rkv = [sb(f"w_rkv{n}", [P, KD, P]) for n in range(2)]
        w_dec, w_rate, w_g = sb("w_dec", [P, P]), sb("w_rate", [P, P]), sb("w_g", [P, P])
        r, k, v_, kk = sb("r_T", [P, TOK]), sb("k_T", [P, TOK]), sb("v_T", [P, TOK]), sb("kk_T", [P, TOK])
        bonus = [sb(f"bonus{n}", [P, TOK]) for n in range(2)]
        sg = [sb(f"sg{n}", [P, TOK]) for n in range(2)]
        rate = [sb(f"rate{n}", [P, TOK]) for n in range(2)]
        G, e1, e2 = sb("G_T", [P, TOK]), sb("e1_T", [P, TOK]), sb("e2_T", [P, TOK])
        AR = [[sb(f"AR{m}{n}", [P, NT, 2, P]) for n in range(2)] for m in range(2)]
        K = [sb(f"K{n}", [P, TOK]) for n in range(2)]
        B = [sb(f"B{n}", [P, TOK]) for n in range(2)]
        Kt = [[sb(f"Kt{m}{n}", [P, NT, P]) for n in range(2)] for m in range(2)]
        Bt = [[sb(f"Bt{m}{n}", [P, NT, P]) for n in range(2)] for m in range(2)]
        Vt = [sb(f"Vt{m}", [P, NT, P]) for m in range(2)]
        half, eT = sb("half_total", [P, 2, NT]), [sb(f"exp_total{m}", [P, 2, 2, NT]) for m in range(2)]
        NRR = sb("NRR", [P, NG * NPROB, 3, P])
        TT, M = [spare[:, n * NG * NPROB * P:(n + 1) * NG * NPROB * P].rearrange("p (g q n) -> p g q n", g=NG, q=NPROB)
                 for n in range(2)]
        T, Z, Mo = sb("T", [P, 2, NPROB, P]), sb("Z", [P, 2, NPROB, P]), sb("Mo", [P, 2, NPROB, P])
        y, yg = [t[:, :, :, :].rearrange("p s q n -> p (s q n)")[:, 0:TOK] for t in (T, Z)]
        state_in = [sb(f"state_in{n}", [P, P]) for n in range(2)]
        S = [[sb(f"S{m}{n}", [P, P]) for n in range(2)] for m in range(2)]
        Sctx, Sdec, Xs = [[sb(f"{x}{n}", [P, P]) for n in range(2)] for x in ("Sctx", "Sdec", "Xs")]
        state_out = sb("state_out", [P, 2, P])
        F = [ctx.enter_context(nc.psum_tensor(f"ps_scan{n}", [P, 1024], F32)) for n in range(4)]
        bank = lambda n: F[n // 2][:, n % 2 * 512:(n % 2 + 1) * 512]
        b_z, b_dt, b_dtt = (lambda s: bank(2 * s)), (lambda s: bank(2 * s + 1)), (lambda s: bank(4 + s))
        b_pair = lambda p: bank((0, 2, 1, 3)[p % 4])
        b_m = lambda h: bank(4 + h)
        b_chain = lambda dr: bank(2 + dr)
        U = lambda dr, c: M[:, c, 2 * dr, :]
        Sp = lambda dr, c: M[:, c, 2 * dr + 1, :]
        wide = ((0, LAT), (LAT, TOK))

        s_const, s_masks, s_parps, s_clear = sem("s_scan_const"), sem("s_masks"), sem("s_par_ps"), sem("s_states_clear")
        s_wr, s_wup, s_wg, s_stin = [sem("s_w_rkv0"), sem("s_w_rkv1")], sem("s_w_up"), sem("s_w_g"), sem("s_state_in")
        s_turn, s_kk = sem("s_turn"), sem("s_kk")
        s_cur, s_job, s_free = sem("s_par_cur"), sem("s_front_mm"), sem("s_front_read")
        s_mid, s_sig, s_sq, s_rt = sem("s_conv_mid"), sem("s_sigmoids"), sem("s_k_squared"), sem("s_norm_root")
        s_conv, s_G, s_e, s_eu, s_kb, s_bon = (sem("s_conv"), sem("s_G"), sem("s_exp"), sem("s_exp_used"), sem("s_kb"),
                                               sem("s_bonus_in"))
        s_front = sem("s_front_done")
        s_a, s_am, s_m, s_ms = sem("s_pair_mm"), sem("s_pair_sb"), sem("s_m_mm"), sem("s_m_sb")
        s_tt0, s_ti, s_mo = sem("s_tt_start"), sem("s_t_start"), sem("s_m_off")
        s_z, s_zs, s_dtt, s_dt, s_tt, s_t = (sem("s_z_mm"), sem("s_z_sb"), sem("s_dtt_mm"), sem("s_dt_mm"), sem("s_tt"),
                                             sem("s_t"))
        s_sp, s_x, s_xs, s_u, s_us, s_sn, s_s = (sem("s_state_scaled"), sem("s_x_mm"), sem("s_x_sb"), sem("s_u_mm"),
                                                 sem("s_u_sb"), sem("s_state_mm"), sem("s_state_next"))
        s_y, s_ys, s_so, s_sos, s_sout = (sem("s_y_mm"), sem("s_y_sb"), sem("s_state_out_tr"), sem("s_state_out_sb"),
                                          sem("s_state_out"))
        s_mu, s_yc, s_ysq, s_g, s_gs, s_var, s_vare, s_std, s_yg, s_ygo = (
            sem("s_mean_mm"), sem("s_y_centred"), sem("s_y_sq"), sem("s_g_mm"), sem("s_g_sb"), sem("s_var_mm"),
            sem("s_var_eps"), sem("s_std"), sem("s_yg"), sem("s_yg_out"))
        block = ctx.enter_context(nc.Block())

        rows = [("conv_w", 0, 0, 72), ("w_decay0", 1, 0, 16), ("a0", 1, 16, 16), ("k_k", 1, 32, 8), ("k_a", 1, 40, 8),
                ("r_k", 1, 48, 8), ("gn_g", 1, 56, 8), ("gn_b", 1, 64, 8)]
        par_rows = Z[:, 0, 0:2, :]
        stage = NRR[:, :, :, :].rearrange("p a b n -> p (a b n)")
        levels_f = stage[:, 0:2 * LEVELS * P].rearrange("p (e l n) -> p e l n", e=2, l=LEVELS)
        causal_f = stage[:, 2 * LEVELS * P:2 * LEVELS * P + 4 * P].rearrange("p (e l n) -> p e l n", e=2, l=2)
        w_in = d["w_in"][0].rearrange("(k p) n -> p k n", p=P)
        N_CONST = len(rows) + 4

        def tiles(eng, body):
            body(0, 0, True, False)
            with eng.Fori(0, (KD - 2) // 2) as j:
                body(2 * j + 1, 1, False, False)
                body(2 * j + 2, 0, False, False)
            body(KD - 1, 1, False, True)

        @block.sync
        def _(sp):
            for name, tile, r0, n in rows:
                a = d[name]
                if name == "r_k":
                    src = a[0].rearrange("(j h) n -> j (h n)", h=2)
                elif len(a.shape) == 3:
                    src = a[0].rearrange("t (j p) -> (t j) p", p=P)
                else:
                    src = a.rearrange("a (j p) -> (a j) p", p=P)
                sp.dma_start(par_rows[r0:r0 + n, tile, :], src).then_inc(s_const, 16)
            sp.dma_start(headones[:, :], d["headones"]).then_inc(s_const, 16)
            sp.dma_start(causal_f, d["causal"]).then_inc(s_const, 16)
            sp.dma_start(levels_f, d["levels"]).then_inc(s_const, 16)
            sp.dma_start(reset[:, :], d["reset"]).then_inc(s_const, 16)

            def await_(signal, value):
                sp.wait_ge(signal, value)
                sp.sem_inc(s_turn, 1)

            def load_rkv(i, n):
                sp.dma_start(w_rkv[n % 2][:, :, :], w_in[:, :, bass.ds(COL_RKV + n * DM + i * P, P)]).then_inc(s_wr[n % 2], 16)

            def loads(i, first=False):
                for n in range(2):
                    if not first:
                        await_(s_job, NJ * (i - 1) + 3 - n)
                    load_rkv(i, n)
                if not first:
                    await_(s_job, NJ * (i - 1) + JOBS.index(J_ST) + 1)
                sp.dma_start(w_dec[:, :], d["w_decay_up"][0].rearrange("e r c -> (e r) c")[:, bass.ts(i, P)]).then_inc(s_wup, 16)
                sp.dma_start(w_rate[:, :], d["a_up"][0].rearrange("e r c -> (e r) c")[:, bass.ts(i, P)]).then_inc(s_wup, 16)
                for dr, src in enumerate((d["state_fwd"], d["state_bwd"])):
                    for h in range(2):
                        sp.dma_start(state_in[dr][h * HD:(h + 1) * HD, h * HD:(h + 1) * HD],
                                     src[0, 0].rearrange("h a b -> (h a) b")[bass.ds(i * P + h * HD, HD), :]).then_inc(s_stin, 16)

            def load_v(i):
                await_(s_job, NJ * i + 1)
                load_rkv(i, 2)

            def load_gate(i):
                sp.dma_start(w_g[:, :], d["g_up"][0][:, bass.ts(i, P)]).then_inc(s_wg, 16)

            def store_states(i):
                await_(s_sos, i + 1)
                for dr, dst in enumerate((d["new_state_fwd"], d["new_state_bwd"])):
                    for h in range(2):
                        sp.dma_start(dst[0, 0].rearrange("h a b -> (h a) b")[bass.ds(i * P + h * HD, HD), :],
                                     state_out[h * HD:(h + 1) * HD, dr, h * HD:(h + 1) * HD]).then_inc(s_sout, 16)

            def store_tile(i):
                await_(s_yg, i + 1)
                sp.dma_start(d["yg"][:, bass.ds(i, 1), :].rearrange("p a n -> p (a n)"), yg).then_inc(s_ygo, 16)

            sp.wait_ge(s_clear, 1)
            loads(0, True)
            load_gate(0)
            load_v(0)
            loads(1)
            load_v(1)
            loads(2)
            with sp.Fori(1, KD - 2) as i:
                store_states(i - 1)
                await_(s_g, i)
                load_gate(i)
                store_tile(i - 1)
                load_v(i + 1)
                loads(i + 2)
            store_states(KD - 3)
            await_(s_g, KD - 2)
            load_gate(KD - 2)
            store_tile(KD - 3)
            load_v(KD - 1)
            store_states(KD - 2)
            await_(s_g, KD - 1)
            load_gate(KD - 1)
            store_tile(KD - 2)
            store_states(KD - 1)
            store_tile(KD - 1)
            sp.wait_ge(s_sout, 64 * KD + 64)
            sp.wait_ge(s_ygo, 16 * KD + 16)

        @block.gpsimd
        def _(g_):
            for dr in range(2):
                g_.memset(state_in[dr][:, :], 0.0)
                g_.memset(Sctx[dr][:, :], 0.0)
            g_.drain().then_inc(s_clear, 1)
            g_.wait_ge(s_masks, 1)

            def body(i, m, first, last):
                def tt_start(n):
                    g = ORDER[n]
                    g_.wait_ge(s_am, (i * NG + n + 1) * NPROB)
                    g_.tensor_tensor(TT[:, g, :, :], TT[:, g, :, :], ident[:, :].unsqueeze(1).broadcast_to([P, NPROB, P]), ALU.add).then_inc(s_tt0, 1)

                def m_off(n):
                    g, l = steps[n]
                    g_.wait_ge(s_ms, i * NG + POS[g] + 1)
                    if slot_before[n] is not None:
                        g_.wait_ge(s_z, i * NS + slot_before[n] + 1)
                    for h in range(2):
                        ins = g_.tensor_tensor(Mo[:, SLOT[g], h::2, :], M[:, g, h::2, :], levels[:, :, l, :], ALU.mult)
                    ins.then_inc(s_mo, 1)

                for n in range(NG - 1):
                    tt_start(n)
                m_off(0)
                m_off(1)
                tt_start(NG - 1)
                for n in range(2, NS):
                    m_off(n)
            tiles(g_, body)

        @block.scalar
        def _(act):
            chunks = lambda t: t.rearrange("p (t n) -> p t n", t=NT)
            ps = F[3][:, 0:TOK]

            def front(n, i, m):
                c = cur[m]
                done = lambda j: act.wait_ge(s_job, NJ * i + JOBS.index(j) + 1)
                if n in (J_R, J_K, J_V):
                    done(n)
                    if n == J_R:
                        act.wait_ge(s_cur, i + 1)
                    act.activation((r, k, v_)[n][:, :], ps, ACT.Copy, scale=c[:, C_CONV1 + n:C_CONV1 + n + 1]).then_inc(s_mid, 1)
                if n in (J_DEC0, J_DEC1, J_RATE0, J_RATE1):
                    dst, col = {J_DEC0: (sg[0], C_DEC0), J_DEC1: (sg[1], C_DEC0 + 1), J_RATE0: (rate[0], C_RATE0),
                                J_RATE1: (rate[1], C_RATE0 + 1)}[n]
                    done(n)
                    act.activation(dst[:, :], ps, ACT.Sigmoid, bias=c[:, col:col + 1]).then_inc(s_free, 1)
                    act.drain().then_inc(s_sig, 1)
                if n == J_DEC0:
                    act.wait_ge(s_conv, 3 * i + 2)
                    act.activation(e2[:, :], k[:, :], ACT.Square, scale=c[:, C_KK:C_KK + 1]).then_inc(s_sq, 1)
                if n == J_DEC1:
                    act.wait_ge(s_rt, 2 * i + 1)
                    act.activation(e2[:, :], e2[:, :], ACT.Sqrt).then_inc(s_rt, 1)
                if n == J_VT:
                    done(n)
                    act.activation(Vt[m][:, :, :], chunks(ps), ACT.Copy).then_inc(s_free, 1)
                if n == J_ST:
                    done(n)
                    act.activation(S[m][0][:, :], ps[:, 0:P], ACT.Copy)
                    act.activation(S[m][1][:, :], ps[:, P:2 * P], ACT.Copy).then_inc(s_free, 1)
                if n in (J_KT0, J_BT0, J_KT1, J_BT1):
                    done(n)
                    dst = {J_KT0: Kt[m][0], J_BT0: Bt[m][0], J_KT1: Kt[m][1], J_BT1: Bt[m][1]}[n]
                    act.activation(dst[:, :, :], chunks(ps), ACT.Copy).then_inc(s_free, 1)
                for at, dr, which in ((J_RATE1, 0, (0, 1)), (J_VT, 0, (2,)), (J_BT0, 1, (0, 1)), (J_NONE1, 1, (2,))):
                    if n != at:
                        continue
                    if which[0] == 0:
                        act.wait_ge(s_G, 2 * i + dr + 1)
                        act.activation(eT[m][:, dr, 0, :], half[:, dr, :], ACT.Exp, scale=-DECAY)
                        act.activation(eT[m][:, dr, 1, :], half[:, dr, :], ACT.Exp, scale=-2 * DECAY)
                    exps = ((G, -DECAY), (sg[0], -DECAY), (G, DECAY)) if dr == 0 else ((sg[1], DECAY), (G, DECAY), (sg[1], -DECAY))
                    for q in which:
                        src, scale = exps[q]
                        e = 3 * dr + q
                        if e == 1:
                            act.wait_ge(s_kk, i + 1)
                        if e >= 2:
                            act.wait_ge(s_eu, 6 * i + e - 1)
                        act.activation((e1, e2)[e % 2][:, :], src[:, :], ACT.Exp, scale=scale).then_inc(s_e, 1)

            def norm(n, i):
                if n == 0:
                    act.wait_ge(s_yc, i + 1)
                    act.activation(e2[:, :], y, ACT.Square).then_inc(s_ysq, 1)
                if n == 1:
                    act.wait_ge(s_vare, i + 1)
                    act.activation(e2[:, :], e2[:, :], ACT.Sqrt).then_inc(s_std, 1)
                if n == 2:
                    act.wait_ge(s_g, i + 1)
                    act.activation(e1[:, :], ps, ACT.Copy).then_inc(s_gs, 1)

            def part(i, n, kind):
                for dr in range(2):
                    c = latent(dr, n) if n < CT else CT
                    if kind == "X":
                        act.wait_ge(s_x, i * 2 * NT + 2 * n + dr + 1)
                        act.activation(Xs[dr][:, :], b_chain(dr)[:, 0:P], ACT.Copy).then_inc(s_xs, 1)
                    if kind == "U":
                        act.wait_ge(s_u, i * 2 * NT + 2 * n + dr + 1)
                        act.activation(U(dr, c), b_chain(dr)[:, P:2 * P], ACT.Copy).then_inc(s_us, 1)

            def body(i, m, first, last):
                for n, g in enumerate(ORDER):
                    act.wait_ge(s_m, i * NG + n + 1)
                    for h in range(2):
                        ins = act.activation(M[:, g, h::2, :], b_m(h)[:, 0:2 * P].rearrange("p (e n) -> p e n", e=2), ACT.Copy)
                    ins.then_inc(s_ms, 1)
                    if not first:
                        norm(n, i - 1)
                for rd, (gs, l) in enumerate(rounds):
                    for a, g in enumerate(gs):
                        n = first_step[rd] + a
                        act.wait_ge(s_z, i * NS + n + 1)
                        if n < 2:
                            act.wait_ge(s_ygo, 16 * i + 16)
                        act.activation(Z[:, SLOT[g], :, :], b_z(SLOT[g]).rearrange("p (q n) -> p q n", q=NPROB), ACT.Copy).then_inc(s_zs, 1)
                    if not last and rd < 17:
                        front(rd, i + 1, 1 - m)
                    for q in (2 * (rd - CH0), 2 * (rd - CH0) + 1):
                        if 0 <= q < len(parts):
                            part(i, *parts[q])
                part(i, CT, "X")
                part(i, CT, "U")
                act.wait_ge(s_y, i + 1)
                act.activation(y, F[0][:, 0:TOK], ACT.Copy).then_inc(s_ys, 1)
                act.wait_ge(s_so, i + 1)
                act.wait_ge(s_sout, 64 * i + 64)
                act.activation(state_out[:, :, :], bank(5)[:, 0:2 * P].rearrange("p (e n) -> p e n", e=2), ACT.Copy).then_inc(s_sos, 1)

            for n in range(17):
                front(n, 0, 0)
            tiles(act, body)
            for n in range(NG):
                norm(n, KD - 1)

        @block.tensor
        def _(pe):
            pe.wait_ge(s_const, 16 * N_CONST)
            for t in range(2):
                last = pe.transpose(F[0][:, t * 72:(t + 1) * 72], par_rows[0:72, t, :], ident[0:72, 0:72])
            last.then_inc(s_parps, 1)

            def front(n, i, m):
                if n not in JOBS:
                    return
                pe.wait_ge(s_free, NJ * i + JOBS.index(n) + 1)
                if n in (J_R, J_K, J_V):
                    pe.wait_ge(s_wr[n % 2], (32 * i + (16, 16, 32)[n]) if n % 2 == 0 else 16 * i + 16)
                    for c0, c1 in wide:
                        for kt in range(KD):
                            last = pe.matmul(F[3][:, c0:c1], w_rkv[n % 2][:, kt, :], hT[:, kt, c0:c1], start=(kt == 0), stop=(kt == KD - 1))
                if n in (J_DEC0, J_DEC1, J_RATE0, J_RATE1):
                    w, x = (w_dec, lora[0]) if n in (J_DEC0, J_DEC1) else (w_rate, lora[1])
                    a = LORA * (n in (J_DEC1, J_RATE1))
                    pe.wait_ge(s_wup, 32 * i + 32)
                    for c0, c1 in wide:
                        last = pe.matmul(F[3][:, c0:c1], w[a:a + LORA, :], x[a:a + LORA, c0:c1], start=True, stop=True)
                if n == J_NORM:
                    pe.wait_ge(s_sq, i + 1)
                    for c0, c1 in wide:
                        last = pe.matmul(F[3][:, c0:c1], headones[:, :], e2[:, c0:c1], start=True, stop=True)
                if n == J_ST:
                    pe.wait_ge(s_stin, 64 * i + 64)
                    for dr in range(2):
                        last = pe.transpose(F[3][:, dr * P:(dr + 1) * P], state_in[dr][:, :], ident[:, :])
                if n in (J_VT, J_KT0, J_BT0, J_KT1, J_BT1):
                    src = {J_VT: v_, J_KT0: K[0], J_BT0: B[0], J_KT1: K[1], J_BT1: B[1]}[n]
                    if n != J_VT:
                        pe.wait_ge(s_kb, 2 * i + 1 + (n in (J_KT1, J_BT1)))
                    for t in range(NT):
                        last = pe.transpose(F[3][:, t * P:(t + 1) * P], src[:, t * P:(t + 1) * P], ident[:, :])
                if n == J_BONUS:
                    pe.wait_ge(s_bon, i + 1)
                    for c0, c1 in wide:
                        last = pe.matmul(F[3][:, c0:c1], headones[:, :], bonus[m][:, c0:c1], start=True, stop=True)
                last.then_inc(s_job, 1)

            def norm(n, i, fronts):
                if n == 0:
                    pe.wait_ge(s_free, NJ * fronts + 1)
                    pe.wait_ge(s_ys, i + 1)
                    for c0, c1 in wide:
                        last = pe.matmul(F[3][:, c0:c1], headmean[:, :], y[:, c0:c1], start=True, stop=True)
                    last.then_inc(s_mu, 1)
                if n == 1:
                    pe.wait_ge(s_yc, i + 1)
                    pe.wait_ge(s_ysq, i + 1)
                    for c0, c1 in wide:
                        last = pe.matmul(F[3][:, c0:c1], headmean[:, :], e2[:, c0:c1], start=True, stop=True)
                    last.then_inc(s_var, 1)
                if n == 2:
                    pe.wait_ge(s_vare, i + 1)
                    pe.wait_ge(s_wg, 16 * i + 16)
                    for c0, c1 in wide:
                        last = pe.matmul(F[3][:, c0:c1], w_g[:, :], lora[2][:, c0:c1], start=True, stop=True)
                    last.then_inc(s_g, 1)

            def pair_products(i, m, n):
                g = ORDER[n]
                for dr in range(2):
                    for h in range(2):
                        p = NPROB * n + 2 * dr + h
                        hs = slice(h * HD, (h + 1) * HD)
                        out = b_pair(p)
                        if p >= 4:
                            pe.wait_ge(s_am, i * NG * NPROB + p - 3)
                        rhs = AR[m][dr][hs, g, :, :]
                        pe.matmul(out[:, 0:2 * P], K[dr][hs, g * P:(g + 1) * P], rhs, start=True, stop=True)
                        pe.matmul(out[:, 2 * P:4 * P], B[dr][hs, g * P:(g + 1) * P], rhs, start=True, stop=True).then_inc(s_a, 1)
                if n >= 1:
                    pe.wait_ge(s_ms, i * NG + n)
                for dr in range(2):
                    for h in range(2):
                        hs = slice(h * HD, (h + 1) * HD)
                        last = pe.matmul(b_m(h)[:, dr * P:(dr + 1) * P], AR[m][dr][hs, g, 0, :],
                                         B[dr][hs, g * P:(g + 1) * P], start=True, stop=True)
                last.then_inc(s_m, 1)

            def z_step(i, n):
                g, l = steps[n]
                s = SLOT[g]
                pe.wait_ge(s_mo, i * NS + n + 1)
                if l == 1:
                    pe.wait_ge(s_tt0, i * NG + POS[g] + 1)
                if slot_before[n] is not None:
                    pe.wait_ge(s_tt, i * NS + slot_before[n] + 1)
                    pe.wait_ge(s_zs, i * NS + slot_before[n] + 1)
                for q in range(NPROB):
                    last = pe.matmul(b_z(s)[:, q * P:(q + 1) * P], Mo[:, s, q, :], TT[:, g, q, :], start=True, stop=True)
                last.then_inc(s_z, 1)

            def t_step(i, n):
                g, l = steps[n]
                s = SLOT[g]
                pe.wait_ge(s_zs, i * NS + n + 1)
                if slot_before[n] is not None:
                    pe.wait_ge(s_t, i * ND + dcount[slot_before[n]])
                if l == 1:
                    pe.wait_ge(s_ti, i * NG + POS[g] + 1)
                for q in range(NPROB):
                    last = pe.matmul(b_dtt(s)[:, q * P:(q + 1) * P], T[:, s, q, :], Z[:, s, q, :], start=True, stop=True)
                last.then_inc(s_dtt, 1)
                if l < LEVELS - 1:
                    for q in range(NPROB):
                        last = pe.matmul(b_dt(s)[:, q * P:(q + 1) * P], Z[:, s, q, :], T[:, s, q, :], start=True, stop=True)
                    last.then_inc(s_dt, 1)

            def part(i, m, n, kind):
                for dr in range(2):
                    c = latent(dr, n) if n < CT else CT
                    p0 = NPROB * POS[c] + 2 * dr
                    X, Ups, Sps = [b_chain(dr)[:, a * P:(a + 1) * P] for a in range(3)]
                    if kind == "X":
                        if c != CT:
                            pe.wait_ge(s_sp, i * 2 * CT + 2 * n + dr + 1)
                        for h in range(2):
                            cs = slice(h * HD, (h + 1) * HD)
                            last = pe.matmul(X[:, cs], NRR[:, p0 + h, 0, :], Vt[m][:, c, cs], start=(c == CT or h == 0), stop=(c == CT),
                                             skip_group_check=True)
                        if c != CT:
                            last = pe.matmul(X, AR[m][dr][:, c, 0, :], Sp(dr, c), start=False, stop=True, skip_group_check=True)
                        last.then_inc(s_x, 1)
                    if kind == "U":
                        pe.wait_ge(s_xs, i * 2 * NT + 2 * n + dr + 1)
                        for h in range(2):
                            cs = slice(h * HD, (h + 1) * HD)
                            last = pe.matmul(Ups[:, cs], TT[:, c, 2 * dr + h, :], Xs[dr][:, cs], start=True, stop=True)
                        last.then_inc(s_u, 1)
                    if kind == "S":
                        pe.wait_ge(s_us, i * 2 * NT + 2 * n + dr + 1)
                        pe.matmul(Sps, Bt[m][dr][:, c, :], U(dr, c), start=True, stop=False)
                        pe.matmul(Sps, Kt[m][dr][:, c, :], Vt[m][:, c, :], start=False, stop=True).then_inc(s_sn, 1)

            def output(m, c):
                Y = F[0][:, c * P:(c + 1) * P]
                for dr in range(2):
                    for h in range(2):
                        p, cs = NPROB * POS[c] + 2 * dr + h, slice(h * HD, (h + 1) * HD)
                        pe.matmul(Y[cs, :], U(dr, c)[:, cs], NRR[:, p, 2, :], start=(dr == 0), stop=False, skip_group_check=True)
                        last = pe.matmul(Y[cs, :], Vt[m][:, c, cs], NRR[:, p, 1, :], start=False, stop=(c == CT and dr == 1),
                                         skip_group_check=True)
                if c != CT:
                    for dr in range(2):
                        last = pe.matmul(Y, Sp(dr, c), AR[m][dr][:, c, 1, :], start=False, stop=(dr == 1), skip_group_check=True)
                return last

            def body(i, m, first, last):
                pe.wait_ge(s_front, i + 1)
                if not first:
                    pe.wait_ge(s_sos, i)
                for n in range(NG):
                    pair_products(i, m, n)
                    if not first:
                        norm(n, i - 1, i + 1)
                pe.wait_ge(s_am, i * NG * NPROB + NG * NPROB)
                pe.wait_ge(s_ms, i * NG + NG)
                if not first:
                    pe.wait_ge(s_gs, i)
                for rd, (gs, l) in enumerate(rounds):
                    here = range(first_step[rd], first_step[rd] + len(gs))
                    q = 2 * (rd - CH0)
                    for n in here:
                        z_step(i, n)
                    if not last and rd < 17:
                        front(rd, i + 1, 1 - m)
                    if 0 <= q < len(parts):
                        if q == 0:
                            pe.wait_ge(s_tt, i * NS + first_step[CH0])
                        part(i, m, *parts[q])
                    for n in here:
                        t_step(i, n)
                    if 0 <= q + 1 < len(parts):
                        part(i, m, *parts[q + 1])
                pe.wait_ge(s_us, i * 2 * NT + 2 * CT)
                part(i, m, CT, "X")
                pe.wait_ge(s_tt, i * NS + NS)
                output(m, 0)
                part(i, m, CT, "U")
                output(m, 1)
                part(i, m, CT, "S")
                output(m, 2)
                output(m, 3)
                output(m, CT).then_inc(s_y, 1)
                pe.wait_ge(s_s, 2 * i + 2)
                for dr in range(2):
                    last_ = pe.transpose(bank(5)[:, dr * P:(dr + 1) * P], Sctx[dr][:, :], ident[:, :])
                last_.then_inc(s_so, 1)

            pe.wait_ge(s_masks, 1)
            for n in range(17):
                front(n, 0, 0)
            tiles(pe, body)
            for n in range(NG):
                norm(n, KD - 1, KD)

        @block.vector
        def _(v):
            chunks = lambda t: t[:, :].rearrange("p (t n) -> p t n", t=NT)
            ps = F[3]
            v.wait_ge(s_parps, 1)
            v.tensor_copy(par[:, :, :], F[0][:, 0:144].rearrange("p (n j) -> p n j", j=KD))
            v.tensor_scalar(headmean[:, :], headones[:, :], 1.0 / HD, None, ALU.mult)
            v.tensor_copy(levels[:, :, :, :], levels_f)
            v.tensor_copy(causal[:, :, :, :], causal_f)
            v.drain().then_inc(s_masks, 1)
            v.sem_inc(s_sout, 64)
            v.sem_inc(s_ygo, 16)
            v.sem_inc(s_free, 1)

            def decays(i, dr, half_):
                if half_ == 0:
                    v.wait_ge(s_sig, 4 * i + (1, 2)[dr])
                    if dr == 1:
                        v.wait_ge(s_e, 6 * i + 3)
                    v.tensor_tensor_scan(G[:, :], reset[:, :], sg[dr][:, :], 0.0, ALU.mult, ALU.add)
                    v.drain()
                    v.tensor_scalar(half[:, dr, :], chunks(G)[:, :, P - 1], 0.5, None, ALU.mult)
                    v.drain()
                else:
                    v.tensor_tensor(chunks(G), chunks(G), half[:, dr, :].unsqueeze(2).broadcast_to([P, NT, P]), ALU.subtract)
                    v.drain()
                    v.tensor_tensor(sg[dr][:, :], G[:, :], sg[dr][:, :], ALU.subtract).then_inc(s_G, 1)

            def keys(i, m, dr):
                v.wait_ge(s_sig, 4 * i + 3 + dr)
                v.tensor_scalar(B[dr][:, :], rate[dr][:, :], -1.0, cur[m][:, C_KA:C_KA + 1], ALU.add, ALU.mult)
                v.tensor_tensor(rate[dr][:, :], kk[:, :], rate[dr][:, :], ALU.mult)
                v.drain()
                v.scalar_tensor_tensor(K[dr][:, :], B[dr][:, :], 1.0, k[:, :], ALU.add, ALU.mult)
                v.drain()
                if dr == 0:
                    v.tensor_copy(bonus[m][:, :], K[0][:, :])
                else:
                    v.tensor_tensor(bonus[m][:, :], bonus[m][:, :], K[1][:, :], ALU.add)

            def operands(i, m, dr, which):
                for n in which:
                    e = (e1, e2)[(3 * dr + n) % 2]
                    v.wait_ge(s_e, 6 * i + 3 * dr + n + 1)
                    if n == 0:
                        ins = v.tensor_tensor(AR[m][dr][:, :, 1, :], chunks(r), chunks(e), ALU.mult)
                    elif n == 1:
                        ins = v.scalar_tensor_tensor(AR[m][dr][:, :, 0, :], chunks(kk), -1.0, chunks(e), ALU.mult, ALU.mult)
                    else:
                        v.tensor_tensor(K[dr][:, :], K[dr][:, :], e[:, :], ALU.mult)
                        ins = v.tensor_tensor(B[dr][:, :], rate[dr][:, :], e[:, :], ALU.mult)
                    ins.then_inc(s_eu, 1)
                if which[-1] == 2:
                    v.drain().then_inc(s_kb, 1)

            def front(n, i, m):
                if n in (J_R, J_K, J_V):
                    if n == J_R:
                        v.tensor_copy(cur[m][:, :], par[:, :, bass.ds(i, 1)].rearrange("p n a -> p (n a)")).then_inc(s_cur, 1)
                    dst = (r, k, v_)[n]
                    v.wait_ge(s_mid, 3 * i + n + 1)
                    if n == 0:
                        v.wait_ge(s_cur, i + 1)
                    for c0, c1 in wide:
                        v.scalar_tensor_tensor(dst[:, c0 + 1:c1], ps[:, c0:c1 - 1], cur[m][:, C_CONV0 + n:C_CONV0 + n + 1],
                                               dst[:, c0 + 1:c1], ALU.mult, ALU.add)
                    v.drain()
                    for c0, c1 in wide:
                        ins = v.scalar_tensor_tensor(dst[:, c0:c1 - 1], ps[:, c0 + 1:c1], cur[m][:, C_CONV2 + n:C_CONV2 + n + 1],
                                                     dst[:, c0:c1 - 1], ALU.mult, ALU.add)
                    ins.then_inc(s_free, 1)
                    v.drain().then_inc(s_conv, 1)
                if n == J_DEC0:
                    decays(i, 0, 0)
                if n == J_NORM:
                    v.wait_ge(s_job, NJ * i + J_NORM + 1)
                    v.tensor_scalar(e2[:, :], ps[:, 0:TOK], KK_EPS, None, ALU.add).then_inc(s_free, 1)
                    v.drain().then_inc(s_rt, 1)
                    decays(i, 0, 1)
                if n == J_DEC1:
                    v.wait_ge(s_rt, 2 * i + 2)
                    v.reciprocal(e2[:, :], e2[:, :])
                    v.drain()
                    v.scalar_tensor_tensor(kk[:, :], k[:, :], cur[m][:, C_KK:C_KK + 1], e2[:, :], ALU.mult, ALU.mult)
                    v.drain().then_inc(s_kk, 1)
                if n == J_RATE0:
                    keys(i, m, 0)
                if n == J_RATE1:
                    operands(i, m, 0, (0, 1))
                if n == J_VT:
                    operands(i, m, 0, (2,))
                if n == J_ST:
                    decays(i, 1, 0)
                if n == J_KT0:
                    decays(i, 1, 1)
                if n == J_BT0:
                    keys(i, m, 1)
                if n == J_NONE0:
                    operands(i, m, 1, (0, 1))
                if n == J_NONE1:
                    operands(i, m, 1, (2,))
                    v.scalar_tensor_tensor(bonus[m][:, :], bonus[m][:, :], cur[m][:, C_RK:C_RK + 1], r[:, :], ALU.mult, ALU.mult).then_inc(s_bon, 1)
                if n == J_BONUS:
                    v.wait_ge(s_job, NJ * i + NJ)
                    v.tensor_tensor(bonus[m][:, :], ps[:, 0:TOK], v_[:, :], ALU.mult).then_inc(s_free, 1)
                    v.drain().then_inc(s_front, 1)

            def norm(n, i, m):
                if n == 0:
                    v.wait_ge(s_mu, i + 1)
                    v.tensor_tensor(y, y, ps[:, 0:TOK], ALU.subtract).then_inc(s_yc, 1)
                if n == 1:
                    v.wait_ge(s_var, i + 1)
                    v.tensor_scalar(e2[:, :], ps[:, 0:TOK], GN_EPS, None, ALU.add).then_inc(s_vare, 1)
                if n == 2:
                    v.wait_ge(s_std, i + 1)
                    v.reciprocal(e2[:, :], e2[:, :])
                    v.drain()
                    v.tensor_tensor(y, y, e2[:, :], ALU.mult)
                    v.drain()
                    v.tensor_scalar(y, y, cur[m][:, C_GNG:C_GNG + 1], cur[m][:, C_GNB:C_GNB + 1], ALU.mult, ALU.add)
                    v.drain()
                    v.tensor_tensor(y, y, bonus[m][:, :], ALU.add)
                if n == 3:
                    v.drain()
                    v.wait_ge(s_gs, i + 1)
                    v.tensor_tensor(yg, y, e1[:, :], ALU.mult).then_inc(s_yg, 1)

            def masks(i, n):
                g = ORDER[n]
                for dr in range(2):
                    for h in range(2):
                        p = NPROB * n + 2 * dr + h
                        src = b_pair(p)
                        v.wait_ge(s_a, i * NG * NPROB + p + 1)
                        v.tensor_tensor(NRR[:, p, 0:2, :], src[:, 0:2 * P].rearrange("p (a n) -> p a n", a=2), causal[:, dr, :, :], ALU.mult)
                        v.tensor_tensor(NRR[:, p, 2, :], src[:, 3 * P:4 * P], causal[:, dr, 1, :], ALU.mult)
                        v.tensor_tensor(TT[:, g, 2 * dr + h, :], src[:, 2 * P:3 * P], levels[:, 1 - dr, 0, :], ALU.mult).then_inc(s_am, 1)

            def t_start(g):
                s = SLOT[g]
                for h in range(2):
                    v.tensor_tensor(T[:, s, h::2, :], M[:, g, h::2, :], levels[:, :, 0, :], ALU.mult)
                v.drain()
                v.tensor_tensor(T[:, s, :, :], T[:, s, :, :], ident[:, :].unsqueeze(1).broadcast_to([P, NPROB, P]), ALU.add).then_inc(s_ti, 1)

            def scaled_state(m, dr, n):
                c = latent(dr, n)
                v.tensor_scalar(Sp(dr, c), S[m][dr][:, :], eT[m][:, dr, 0, c:c + 1], None, ALU.mult).then_inc(s_sp, 1)
                v.tensor_scalar(Sdec[dr][:, :], S[m][dr][:, :], eT[m][:, dr, 1, c:c + 1], None, ALU.mult)

            def state(i, m, n):
                for dr in range(2):
                    c = latent(dr, n) if n < CT else CT
                    v.drain()
                    v.wait_ge(s_sn, i * 2 * CT + (2 * n if n < CT else 2 * CT - 2) + dr + 1)
                    for h in range(2):
                        hs = slice(h * HD, (h + 1) * HD)
                        src, e = b_chain(dr)[hs, 2 * P + h * HD:2 * P + (h + 1) * HD], eT[m][hs, dr, 0, c:c + 1]
                        if c == CT:
                            ins = v.tensor_scalar(Sctx[dr][hs, hs], src, e, None, ALU.mult)
                        else:
                            v.scalar_tensor_tensor(S[m][dr][hs, hs], src, e, Sdec[dr][hs, hs], ALU.mult, ALU.add)
                    if c == CT:
                        ins.then_inc(s_s, 1)
                    else:
                        v.drain()
                        scaled_state(m, dr, n + 1)

            def body(i, m, first, last):
                for n in range(NG):
                    if n == NG - 1:
                        v.drain()
                        for g in ORDER[0:2]:
                            v.wait_ge(s_ms, i * NG + POS[g] + 1)
                            t_start(g)
                    masks(i, n)
                    if not first:
                        norm(n, i - 1, 1 - m)
                v.wait_ge(s_ms, i * NG + NG)
                for rd, (gs, l) in enumerate(rounds):
                    q = 2 * (rd - CH0)
                    if 0 <= q < len(parts) and parts[q][1] == "S":
                        state(i, m, parts[q][0])
                    for a, g in enumerate(gs):
                        n = first_step[rd] + a
                        s = SLOT[g]
                        v.wait_ge(s_dtt, i * NS + n + 1)
                        v.tensor_tensor(TT[:, g, :, :], TT[:, g, :, :], b_dtt(s).rearrange("p (q n) -> p q n", q=NPROB), ALU.add).then_inc(s_tt, 1)
                        if l < LEVELS - 1:
                            v.wait_ge(s_dt, i * ND + dcount[n])
                            v.tensor_tensor(T[:, s, :, :], T[:, s, :, :], b_dt(s).rearrange("p (q n) -> p q n", q=NPROB), ALU.add).then_inc(s_t, 1)
                        if l == LEVELS - 1 and POS[g] + 2 < NG:
                            t_start(ORDER[POS[g] + 2])
                    if rd == CH0 - 1:
                        for dr in range(2):
                            scaled_state(m, dr, 0)
                    if 0 <= q + 1 < len(parts) and parts[q + 1][1] == "S":
                        state(i, m, parts[q + 1][0])
                    if not last and rd < 17:
                        front(rd, i + 1, 1 - m)
                state(i, m, CT)

            for n in range(17):
                front(n, 0, 0)
            tiles(v, body)
            for n in range(NG):
                norm(n, KD - 1, 1)


def merge_phase(nc, d, ident, hT, x1, h2, affT, posT):
    G1, SH2, SC2 = 2 * DM, 3 * DM, 4 * DM
    with ExitStack() as ctx:
        sb = lambda n, s: ctx.enter_context(nc.sbuf_tensor(n, s, F32))
        sem = lambda n: ctx.enter_context(nc.semaphore(n))
        fT, ygT = sb("fourierT", [P, FG, TOK]), sb("ygT", [P, KD, TOK])
        PARTS = ((KD, hT), (KD, hT), (FG, fT), (KD, ygT))
        w = [[sb(f"w_merge{j}_{n}", [P, kt, P]) for n, (kt, _) in enumerate(PARTS)] for j in range(2)]
        w_out = sb("w_out_sb", [P, KD, DM])
        mT = sb("mergedT", [P, KD, TOK])
        gate = [sb(f"gate_sb{n}", [P, TOK]) for n in range(2)]
        g1b = [sb(f"gate1_{j}", [P, DM]) for j in range(2)]
        sc2 = [sb(f"scale2_{j}", [P, DM]) for j in range(2)]
        sh2 = [sb(f"shift2_{j}", [P, DM]) for j in range(2)]
        lng, lnb = sb("ln1_g_sb", [P, DM]), sb("ln1_b_sb", [P, DM])
        stats, mv = sb("ln1_stats", [P, 2, 6]), sb("ln1_mv", [P, 4])
        w_r = sb("w_router_sb", [P, KD, NE])
        sm = sb("softmax_stats", [P, 4])
        h2T = [w[j][0] for j in range(2)]
        work, mask, pos, ones = [w[j][n][0:NE, :, :].rearrange("p k n -> p (k n)")[:, 0:TOK] for j in range(2) for n in (1, 3)]
        top8 = sb("top8", [NE, 8])
        F = [ctx.enter_context(nc.psum_tensor(f"ps_merge{n}", [P, 1024], F32)) for n in range(4)]
        s_w, s_wo, s_vec, s_x = [sem("s_w_merge0"), sem("s_w_merge1")], sem("s_w_out"), sem("s_vec"), sem("s_x_again")
        s_mm, s_gate, s_mt = sem("s_merge_mm"), sem("s_gate_sb"), sem("s_mergedT")
        s_o, s_osb, s_st, s_sd, s_x1 = sem("s_out_mm"), sem("s_mix_added"), sem("s_ln1_var"), sem("s_ln1_std"), sem("s_x1")
        s_h2t, s_h2s, s_lg, s_mx, s_ex, s_af = (sem("s_h2_tr"), sem("s_h2T"), sem("s_logits"), sem("s_logit_max"),
                                                sem("s_exp_logits"), sem("s_aff_tok"))
        s_at, s_pos, s_pt, s_h2 = sem("s_aff_tr"), sem("s_slots"), sem("s_slots_tr"), sem("s_h2")
        s_in = [sem("s_fourierT"), sem("s_ygT")]
        block = ctx.enter_context(nc.Block())
        w_in = d["w_in"][0].rearrange("(k p) n -> p k n", p=P)
        w_src = [(w_in, COL_GATE), (w_in, COL_GATE + DM), (d["w_fo"][0].rearrange("(k p) n -> p k n", p=P), 0),
                 (d["w_ro"][0].rearrange("(k p) n -> p k n", p=P), 0)]

        @block.sync
        def _(sp):
            def load(i, j):
                for n, (src, col) in enumerate(w_src):
                    sp.dma_start(w[j][n][:, :, :], src[:, :, bass.ds(col + (2 * i + j) * P, P)]).then_inc(s_w[j], 16)
            load(0, 0)
            sp.dma_start(fT[:, :, :], d["fT"]).then_inc(s_in[0], 16)
            sp.dma_start(ygT[:, :, :], d["yg"]).then_inc(s_in[1], 16)
            load(0, 1)
            sp.dma_start(w_out[:, :, :], d["w_out"][0].rearrange("(k p) n -> p k n", p=P)).then_inc(s_wo, 16)
            sp.dma_start(w_r[:, :, :], d["w_router"][0].rearrange("(k p) n -> p k n", p=P)).then_inc(s_wo, 16)
            for t in range(NT):
                src = d["x_sample"][0, t * P:(t + 1) * P, :] if t < CT else d["x_prompt"][0]
                sp.dma_start(x1[:, t, :], src).then_inc(s_x, 16)
            for j in range(2):
                for dst, col in ((g1b, G1), (sc2, SC2), (sh2, SH2)):
                    sp.dma_start(dst[j][:, :], d["mod"][j:j + 1, col:col + DM].to_broadcast([P, DM])).then_inc(s_vec, 16)
            sp.dma_start(lng[:, :], d["ln1_g"].to_broadcast([P, DM])).then_inc(s_vec, 16)
            sp.dma_start(lnb[:, :], d["ln1_b"].to_broadcast([P, DM])).then_inc(s_vec, 16)
            with sp.Fori(1, KD // 2) as i:
                for j in range(2):
                    sp.wait_ge(s_mm, 8 * i + 4 * j - 4)
                    load(i, j)
            for t in range(NT):
                sp.wait_ge(s_h2, t + 1)
                sp.dma_start(d["x1"][t * P:(t + 1) * P, :], x1[:, t, :]).then_inc(s_x1, 16)
            sp.wait_ge(s_x1, 16 * NT)

        @block.scalar
        def _(act):
            with act.Fori(0, KD // 2) as i:
                for j in range(2):
                    act.wait_ge(s_mt, 2 * i + j + 1)
                    for n in range(2):
                        act.wait_ge(s_mm, 8 * i + 4 * j + n + 1)
                        act.activation(gate[n][:, :], F[n][:, 0:TOK], ACT.Sigmoid).then_inc(s_gate, 1)
            for t in range(NT):
                act.wait_ge(s_st, t + 1)
                act.activation(mv[:, 2:3], mv[:, 2:3], ACT.Sqrt).then_inc(s_sd, 1)
            for t in range(NT):
                act.wait_ge(s_h2t, t + 1)
                if t >= 2:
                    act.wait_ge(s_lg, t - 1)
                act.activation(h2T[t % 2][:, :, :], F[t % 2][:, :].rearrange("p (k n) -> p k n", k=KD), ACT.Copy).then_inc(s_h2s, 1)
            for t in range(NT):
                act.wait_ge(s_mx, t + 1)
                act.activation(affT[:, t, 0:NE], F[2][:, t * NE:(t + 1) * NE], ACT.Exp, bias=sm[:, 0:1],
                               accum_out=sm[:, 1:2]).then_inc(s_ex, 1)

        @block.tensor
        def _(pe):
            with pe.Fori(0, KD // 2) as i:
                for j in range(2):
                    pe.wait_ge(s_w[j], 64 * i + 64)
                    pe.wait_ge(s_mt, 2 * i + j + 1)
                    for n, (kt, x) in enumerate(PARTS):
                        if n >= 2 and j == 0:
                            pe.wait_ge(s_in[n - 2], 16)
                        for c0, c1 in ((0, LAT), (LAT, TOK)):
                            for k in range(kt):
                                last = pe.matmul(F[n][:, c0:c1], w[j][n][:, k, :], x[:, k, c0:c1], start=(k == 0), stop=(k == kt - 1))
                        last.then_inc(s_mm, 1)
            pe.wait_ge(s_mt, KD + 1)
            pe.wait_ge(s_wo, 32)
            for t in range(NT):
                if t >= 2:
                    pe.wait_ge(s_osb, t - 1)
                for n in range(2):
                    for k in range(KD):
                        last = pe.matmul(F[2 + t % 2][:, n * 512:(n + 1) * 512], mT[:, k, t * P:(t + 1) * P],
                                         w_out[:, k, n * 512:(n + 1) * 512], start=(k == 0), stop=(k == KD - 1))
                last.then_inc(s_o, 1)
            pe.wait_ge(s_osb, NT)
            for t in range(NT):
                pe.wait_ge(s_h2, t + 1)
                if t >= 2:
                    pe.wait_ge(s_h2s, t - 1)
                for k in range(KD):
                    last = pe.transpose(F[t % 2][:, k * P:(k + 1) * P], h2[:, t, k * P:(k + 1) * P], ident[:, :])
                last.then_inc(s_h2t, 1)
                pe.wait_ge(s_h2s, t + 1)
                for k in range(KD):
                    last = pe.matmul(F[2][:, t * NE:(t + 1) * NE], h2T[t % 2][:, k, :], w_r[:, k, :], start=(k == 0), stop=(k == KD - 1))
                last.then_inc(s_lg, 1)
            pe.wait_ge(s_af, 1)
            for t in range(NT):
                last = pe.transpose(F[3][0:NE, t * P:(t + 1) * P], affT[:, t, 0:NE], ident[:, :])
            last.then_inc(s_at, 1)
            pe.wait_ge(s_pos, 1)
            for t in range(NT):
                last = pe.transpose(F[2][:, 512 + t * NE:512 + (t + 1) * NE], pos[:, t * P:(t + 1) * P], ident[0:NE, 0:NE])
            last.then_inc(s_pt, 1)

        @block.vector
        def _(v):
            v.sem_inc(s_mt, 1)
            with v.Fori(0, KD // 2) as i:
                for j in range(2):
                    for n in range(2):
                        v.wait_ge(s_gate, 4 * i + 2 * j + n + 1)
                        v.wait_ge(s_mm, 8 * i + 4 * j + n + 3)
                        v.tensor_tensor(gate[n][:, :], gate[n][:, :], F[2 + n][:, 0:TOK], ALU.mult)
                    v.drain()
                    v.tensor_tensor(mT[:, bass.ds(2 * i + j, 1), :].rearrange("p a n -> p (a n)"), gate[0][:, :], gate[1][:, :],
                                    ALU.add).then_inc(s_mt, 1)
            v.wait_ge(s_vec, 16 * 8)
            v.wait_ge(s_x, 16 * NT)
            for j in range(2):
                v.tensor_scalar(sc2[j][:, :], sc2[j][:, :], 1.0, None, ALU.add)
            for t in range(NT):
                j = t // CT
                y = h2[:, t, :]
                v.wait_ge(s_o, t + 1)
                v.tensor_tensor(y, F[2 + t % 2][:, :], g1b[j][:, :], ALU.mult).then_inc(s_osb, 1)
                v.drain()
                v.scalar_tensor_tensor(x1[:, t, :], x1[:, t, :], ALPHA, y, ALU.mult, ALU.add)
                v.drain()
                for n in range(2):
                    v.bn_stats(stats[:, n, :], x1[:, t, n * 512:(n + 1) * 512])
                v.drain()
                v.bn_aggr(mv[:, 0:2], stats[:, :, :])
                v.drain()
                v.tensor_scalar(mv[:, 2:3], mv[:, 1:2], LN_EPS, None, ALU.add).then_inc(s_st, 1)
                v.wait_ge(s_sd, t + 1)
                v.reciprocal(mv[:, 3:4], mv[:, 2:3])
                v.drain()
                v.tensor_scalar(x1[:, t, :], x1[:, t, :], mv[:, 0:1], mv[:, 3:4], ALU.subtract, ALU.mult)
                v.drain()
                v.tensor_tensor(x1[:, t, :], x1[:, t, :], lng[:, :], ALU.mult)
                v.drain()
                v.tensor_tensor(x1[:, t, :], x1[:, t, :], lnb[:, :], ALU.add)
                v.drain()
                v.tensor_tensor(y, x1[:, t, :], sc2[j][:, :], ALU.mult)
                v.drain()
                v.tensor_tensor(y, y, sh2[j][:, :], ALU.add).then_inc(s_h2, 1)
            for t in range(NT):
                if t == 0:
                    v.wait_ge(s_lg, NT)
                v.tensor_reduce(sm[:, 2:3], F[2][:, t * NE:(t + 1) * NE], mybir.AxisListType.X, ALU.max)
                v.drain()
                v.tensor_scalar(sm[:, 0:1], sm[:, 2:3], -1.0, None, ALU.mult).then_inc(s_mx, 1)
                v.wait_ge(s_ex, t + 1)
                v.reciprocal(sm[:, 3:4], sm[:, 1:2])
                v.drain()
                v.tensor_scalar(affT[:, t, 0:NE], affT[:, t, 0:NE], sm[:, 3:4], None, ALU.mult)
            v.drain().then_inc(s_af, 1)
            v.wait_ge(s_at, 1)
            v.memset(ones[:, :], 1.0)
            v.tensor_copy(work[:, :], F[3][0:NE, 0:TOK])
            v.drain()
            for c0, c1, cap in ((0, LAT, CAP_L), (LAT, TOK, CAP_C)):
                for _ in range(cap // 8):
                    v.max(top8[:, :], work[:, c0:c1])
                    v.drain()
                    v.match_replace(work[:, c0:c1], top8[:, :], work[:, c0:c1], -1.0)
                    v.drain()
            v.tensor_scalar(mask[:, :], work[:, :], 0.0, None, ALU.is_lt)
            v.drain()
            for c0, c1 in ((0, LAT), (LAT, TOK)):
                v.tensor_tensor_scan(pos[:, c0:c1], ones[:, c0:c1], mask[:, c0:c1], float(CAP_L if c0 else 0), ALU.mult, ALU.add)
            v.drain()
            v.tensor_tensor(pos[:, :], pos[:, :], mask[:, :], ALU.mult).then_inc(s_pos, 1)
            v.wait_ge(s_pt, 1)
            v.tensor_copy(posT[:, :, 0:NE], F[2][:, 512:512 + NT * NE].rearrange("p (t e) -> p t e", t=NT))


def expert_phase(nc, d, ident, h2, affT, posT):
    NST, FK, NR = 2 * FQ, FW // P, NE // 2
    W1, W3, W2 = range(3)
    with ExitStack() as ctx:
        sb = lambda n, s, dt=F32: ctx.enter_context(nc.sbuf_tensor(n, s, dt))
        sem = lambda n: ctx.enter_context(nc.semaphore(n))
        pair = lambda n, s: [sb(f"{n}_{x}", s, F32R) for x in ("hi", "lo")]
        shape = [[P, KD, FW], [P, KD, FW], [P, FK, DM]]
        raw = [sb(f"w{n}_raw", sh) for n, sh in zip((1, 3, 2), shape)]
        wt = [pair(f"w{n}", sh) for n, sh in zip((1, 3, 2), shape)]
        iota, tokid = sb("iota_slot_sb", [P, CAP]), sb("tok_id_sb", [P, NT])
        cur, colv = sb("slot_cur", [P, NT, 2]), sb("gate_tok", [P, NT, 2, 2])
        sel_l, sel_c = sb("sel_lat", [P, CT, 2, CAP_L]), sb("sel_ctx", [P, 2, CAP_C])
        xT = [pair(f"xT{j}", [P, KD, CAP]) for j in range(2)]
        xN = pair("xT_next", [P, KD, CAP])
        gt = [sb(f"gate_slot{j}", [CAP, 2]) for j in range(2)]
        gN = sb("gate_slot_next", [CAP, 2])
        hs = [sb(f"hidden{j}", [CAP, FW]) for j in range(2)]
        hT = pair("hiddenT", [P, FK, CAP])
        ye = [sb(f"ye{j}", [CAP, DM + 2]) for j in range(2)]
        psH = [ctx.enter_context(nc.psum_tensor(f"ps_h{j}", [P, 1024], F32)) for j in range(2)]
        psY = ctx.enter_context(nc.psum_tensor("ps_y", [P, 1024], F32))
        psT = ctx.enter_context(nc.psum_tensor("ps_t", [P, 512], F32))
        psG = ctx.enter_context(nc.psum_tensor("ps_gather", [P, 512], F32))
        s_raw, s_hi, s_lo = [[sem(f"s_w{n}_{x}") for n in (1, 3, 2)] for x in ("landed", "hi", "split")]
        s_used = [sem("s_w1_used"), sem("s_w3_used"), sem("s_w2_used")]
        s_cst, s_turn = sem("s_moe_const"), sem("s_load_turn")
        s_sel, s_ga, s_xt, s_x1 = sem("s_sel"), sem("s_gather_mm"), sem("s_gathered"), sem("s_xT1")
        s_sg, s_hh, s_tr, s_hth, s_ht, s_ye = (sem("s_sigmoid"), sem("s_hidden"), sem("s_hidden_tr"),
                                               sem("s_hiddenT_hi"), sem("s_hiddenT"), sem("s_ye"))
        s_out = [sem("s_ye_out0"), sem("s_ye_out1")]
        block = ctx.enter_context(nc.Block())
        views = [d["w_e1"][0].rearrange("e (k p) f -> p e k f", p=P), d["w_e3"][0].rearrange("e (k p) f -> p e k f", p=P),
                 d["w_e2"][0].rearrange("e (f p) n -> p e f n", p=P)]
        NG_ = KD // 2

        def rounds(eng, body):
            body(0, True, False)
            with eng.Fori(1, NR - 1) as i:
                body(i, False, False)
            body(NR - 1, False, True)

        @block.sync
        def _(sp):
            sp.dma_start(iota[:, :], d["iota_slot"]).then_inc(s_cst, 16)
            sp.dma_start(tokid[:, :], d["tok_id"]).then_inc(s_cst, 16)

            def load(w, i, s):
                e = bass.ds(2 * i + s // FQ, 1)
                q = s % FQ
                src = views[w][:, e, :, q * FW:(q + 1) * FW] if w != W2 else views[w][:, e, q * FK:(q + 1) * FK, :]
                sp.dma_start(raw[w][:, :, :], src.rearrange("p a k f -> p (a k) f")).then_inc(s_raw[w], 16)

            def store(i, j):
                sp.wait_ge(s_ye, 2 * i + j + 2)
                sp.dma_start(d["ye"][bass.ds((2 * i + j) * CAP, CAP), :], ye[j][:, :]).then_inc(s_out[j], 16)

            def body(i, first, last):
                for s in range(NST):
                    if not (last and s == NST - 1):
                        for w in (W1, W3):
                            sp.wait_ge(s_lo[w], NST * i + s + 1)
                            load(w, i + (s + 1) // NST, (s + 1) % NST)
                    if not (first and s == 0):
                        sp.wait_ge(s_lo[W2], NST * i + s)
                        sp.sem_inc(s_turn, 1)
                    load(W2, i, s)
                    if s == 2 and not first:
                        store(i - 1, 1)
                    if s == FQ + 2:
                        store(i, 0)

            load(W1, 0, 0)
            load(W3, 0, 0)
            rounds(sp, body)
            store(NR - 1, 1)
            for j in range(2):
                sp.wait_ge(s_out[j], 16 * NR + 16)

        @block.scalar
        def _(act):
            def high(w, i, s):
                act.wait_ge(s_raw[w], 16 * (NST * i + s) + 16)
                if not (isinstance(i, int) and NST * i + s == 0):
                    act.wait_ge(s_used[w], NST * i + s)
                act.activation(wt[w][0][:, :, :], raw[w][:, :, :], ACT.Copy).then_inc(s_hi[w], 1)

            def gated(i, j):
                act.wait_ge(s_used[W2], NST * i + (j + 1) * FQ)
                act.wait_ge(s_out[j], 16 * i + 16)
                act.activation(ye[j][:, DM:DM + 2], gt[j][:, :], ACT.Copy)
                act.activation(ye[j][:, 0:DM], psY[0:CAP, :], ACT.Copy, scale=gt[j][:, 0:1]).then_inc(s_ye, 1)

            def body(i, first, last):
                for s in range(NST):
                    more = not (last and s == NST - 1)
                    if more:
                        high(W1, i, s + 1)
                    act.wait_ge(s_used[W3], NST * i + s + 1)
                    act.wait_ge(s_tr, NST * i + s + 1)
                    act.activation(hs[s % 2][:, :], psH[s % 2][0:CAP, 0:FW], ACT.Sigmoid).then_inc(s_sg, 1)
                    if more:
                        high(W3, i, s + 1)
                    if s == 0 and not first:
                        gated(i - 1, 1)
                    if s == FQ:
                        gated(i, 0)
                    high(W2, i, s)
                    act.wait_ge(s_tr, NST * i + s + 3)
                    act.activation(hT[0][:, :, :], psT[:, 0:FK * CAP].rearrange("p (f c) -> p f c", c=CAP), ACT.Copy).then_inc(s_hth, 1)

            high(W1, 0, 0)
            high(W3, 0, 0)
            rounds(act, body)
            gated(NR - 1, 1)

        @block.tensor
        def _(pe):
            def gather(n, m):
                if m == 0:
                    pe.wait_ge(s_sel, n + 1)
                else:
                    pe.wait_ge(s_xt, NG_ * n + m)
                for a in range(2):
                    k = 2 * m + a
                    out = psG[:, a * 2 * CAP:(a + 1) * 2 * CAP].rearrange("p (e c) -> p e c", e=2)
                    for t in range(CT):
                        pe.matmul(out[:, :, 0:CAP_L], h2[:, t, k * P:(k + 1) * P], sel_l[:, t, :, :],
                                  start=(t == 0), stop=(t == CT - 1))
                    last = pe.matmul(out[:, :, CAP_L:CAP], h2[:, CT, k * P:(k + 1) * P], sel_c[:, :, :], start=True, stop=True)
                if m == NG_ - 1:
                    for j in range(2):
                        o = 4 * CAP + 2 * j
                        for t in range(CT):
                            pe.matmul(psG[0:CAP_L, o:o + 2], sel_l[:, t, j, :], colv[:, t, j, :], start=(t == 0), stop=(t == CT - 1))
                        last = pe.matmul(psG[CAP_L:CAP, o:o + 2], sel_c[:, j, :], colv[:, CT, j, :], start=True, stop=True)
                last.then_inc(s_ga, 1)

            def split_product(out, x, w, k, ks, first, last_):
                pe.matmul(out, x[0][:, k, :], w[0][:, k, ks], start=first, stop=False, skip_group_check=True)
                pe.matmul(out, x[0][:, k, :], w[1][:, k, ks], start=False, stop=False, skip_group_check=True)
                return pe.matmul(out, x[1][:, k, :], w[0][:, k, ks], start=False, stop=last_, skip_group_check=True)

            def hidden(w, i, s):
                pe.wait_ge(s_lo[w], NST * i + s + 1)
                if w == W1:
                    pe.wait_ge(s_hh, NST * i + s + 1)
                    if s == 0:
                        pe.wait_ge(s_xt, NG_ * (i + 1))
                    if s == FQ:
                        pe.wait_ge(s_x1, i + 1)
                out = psH[s % 2][0:CAP, 0:FW] if w == W1 else psH[s % 2][0:CAP, FW:2 * FW]
                for k in range(KD):
                    last = split_product(out, xT[s // FQ], wt[w], k, slice(0, FW), k == 0, k == KD - 1)
                last.then_inc(s_used[w], 1)

            def turn(i, s):
                pe.wait_ge(s_hh, NST * i + s + 3)
                pe.wait_ge(s_ht, NST * i + s + 1)
                for f in range(FK):
                    last = pe.transpose(psT[:, f * CAP:(f + 1) * CAP], hs[s % 2][:, f * P:(f + 1) * P], ident[0:CAP, 0:CAP])
                last.then_inc(s_tr, 1)

            def output(i, s):
                pe.wait_ge(s_ht, NST * i + s + 2)
                pe.wait_ge(s_lo[W2], NST * i + s + 1)
                if s % FQ == 0:
                    pe.wait_ge(s_ye, 2 * i + s // FQ + 1)
                for f in range(FK):
                    for n in range(2):
                        last = split_product(psY[0:CAP, n * 512:(n + 1) * 512], hT, wt[W2], f, slice(n * 512, (n + 1) * 512),
                                             s % FQ == 0 and f == 0, s % FQ == FQ - 1 and f == FK - 1)
                last.then_inc(s_used[W2], 1)

            def body(i, first, last):
                for s in range(NST):
                    before = (i, s - 1) if s else None if first else (i - 1, NST - 1)
                    hidden(W1, i, s)
                    if before:
                        turn(*before)
                    hidden(W3, i, s)
                    if s >= FQ and not last:
                        gather(i + 1, s - FQ)
                    if before:
                        output(*before)

            for m in range(NG_):
                gather(0, m)
            rounds(pe, body)
            turn(NR - 1, NST - 1)
            output(NR - 1, NST - 1)

        @block.vector
        def _(v):
            def low(w, i, s):
                v.wait_ge(s_hi[w], NST * i + s + 1)
                v.tensor_tensor(wt[w][1][:, :, :], raw[w][:, :, :], wt[w][0][:, :, :], ALU.subtract).then_inc(s_lo[w], 1)

            def select(n):
                v.tensor_copy(cur[:, :, :], posT[:, :, bass.ds(2 * n, 2)])
                v.tensor_copy(colv[:, :, :, 0], affT[:, :, bass.ds(2 * n, 2)])
                v.drain()
                v.tensor_tensor(sel_l[:, :, :, :].rearrange("p t e c -> p (t e) c"),
                                iota[:, 0:CAP_L].unsqueeze(1).broadcast_to([P, 2 * CT, CAP_L]),
                                cur[:, 0:CT, :].rearrange("p t e -> p (t e)").unsqueeze(2).broadcast_to([P, 2 * CT, CAP_L]), ALU.is_equal)
                v.tensor_tensor(sel_c[:, :, :], iota[:, CAP_L:CAP].unsqueeze(1).broadcast_to([P, 2, CAP_C]),
                                cur[:, CT, :].unsqueeze(2).broadcast_to([P, 2, CAP_C]), ALU.is_equal).then_inc(s_sel, 1)

            def gathered(n, m):
                v.wait_ge(s_ga, NG_ * n + m + 1)
                src = psG[:, 0:4 * CAP].rearrange("p (k e c) -> p k e c", k=2, e=2)
                ks = slice(2 * m, 2 * m + 2)
                for j, dst in enumerate((xT[0], xN)):
                    v.tensor_copy(dst[0][:, ks, :], src[:, :, j, :])
                v.drain()
                for j, dst in enumerate((xT[0], xN)):
                    ins = v.tensor_tensor(dst[1][:, ks, :], src[:, :, j, :], dst[0][:, ks, :], ALU.subtract)
                if m == NG_ - 1:
                    v.tensor_copy(gt[0][:, :], psG[0:CAP, 4 * CAP:4 * CAP + 2])
                    ins = v.tensor_copy(gN[:, :], psG[0:CAP, 4 * CAP + 2:4 * CAP + 4])
                ins.then_inc(s_xt, 1)

            def body(i, first, last):
                for s in range(NST):
                    more = not (last and s == NST - 1)
                    if more:
                        low(W1, i, s + 1)
                    if s == 1:
                        v.wait_ge(s_used[W3], NST * i + 1)
                        v.tensor_copy(xT[1][0][:, :, :], xN[0][:, :, :])
                        v.tensor_copy(xT[1][1][:, :, :], xN[1][:, :, :]).then_inc(s_x1, 1)
                    if s == 2:
                        v.wait_ge(s_ye, 2 * i + 1)
                        v.tensor_copy(gt[1][:, :], gN[:, :])
                    if s == FQ - 1 and not last:
                        select(i + 1)
                    v.wait_ge(s_sg, NST * i + s + 1)
                    v.tensor_tensor(hs[s % 2][:, :], hs[s % 2][:, :], psH[s % 2][0:CAP, 0:FW], ALU.mult)
                    v.drain()
                    v.tensor_tensor(hs[s % 2][:, :], hs[s % 2][:, :], psH[s % 2][0:CAP, FW:2 * FW], ALU.mult).then_inc(s_hh, 1)
                    if more:
                        low(W3, i, s + 1)
                    if s >= FQ and not last:
                        gathered(i + 1, s - FQ)
                    low(W2, i, s)
                    v.wait_ge(s_hth, NST * i + s + 1)
                    v.tensor_tensor(hT[1][:, :, :], psT[:, 0:FK * CAP].rearrange("p (f c) -> p f c", c=CAP), hT[0][:, :, :],
                                    ALU.subtract).then_inc(s_ht, 1)

            v.wait_ge(s_cst, 32)
            for j in range(2):
                v.tensor_copy(colv[:, :, j, 1], tokid[:, :])
                v.sem_inc(s_out[j], 16)
            v.sem_inc(s_hh, 2)
            v.sem_inc(s_tr, 2)
            v.sem_inc(s_ht, 1)
            v.sem_inc(s_ye, 1)
            select(0)
            for m in range(NG_):
                gathered(0, m)
            low(W1, 0, 0)
            low(W3, 0, 0)
            rounds(v, body)


def combine_phase(nc, d):
    G2 = 5 * DM
    ML, MC = NE * CAP_L // P, NE * CAP_C // P
    MT, PER = MC + ML, P // CAP_C
    ROWS = [CT] + list(range(CT))
    with ExitStack() as ctx:
        sb = lambda n, s, dt=F32: ctx.enter_context(nc.sbuf_tensor(n, s, dt))
        sem = lambda n: ctx.enter_context(nc.semaphore(n))
        x1, iota = sb("x1_again", [P, NT, DM]), sb("iota_tok_sb", [P, TOK])
        yt, hot = sb("ye_tiles", [P, MT, DM + 2]), sb("one_hot", [P, MT, LAT], F32R)
        yh, yl = [sb(f"ye_{x}", [P, MT, DM], F32R) for x in ("hi", "lo")]
        g2b = [sb(f"gate2_{j}", [P, DM]) for j in range(2)]
        lng, lnb = sb("ln2_g_sb", [P, DM]), sb("ln2_b_sb", [P, DM])
        mix = [yt[:, t, 0:DM] for t in range(2)]
        stats, mv = sb("ln2_stats", [P, 2, 6]), sb("ln2_mv", [P, 4])
        F = [ctx.enter_context(nc.psum_tensor(f"ps_comb{n}", [P, 1024], F32)) for n in range(4)]
        s_t, s_iota = [sem(f"s_ye_tiles{m}") for m in range(MT // 2)], sem("s_iota")
        s_g2, s_vec = sem("s_gate2_ctx"), sem("s_vec2")
        s_hi, s_hot, s_mm, s_rd, s_st, s_sd, s_nm, s_fin, s_out = (
            sem("s_ye_hi"), sem("s_one_hot"), sem("s_comb_mm"), sem("s_comb_read"), sem("s_ln2_var"), sem("s_ln2_std"),
            sem("s_ln2_normed"), sem("s_final"), sem("s_final_out"))
        block = ctx.enter_context(nc.Block())

        @block.sync
        def _(sp):
            sp.dma_start(iota[:, :], d["iota_tok"]).then_inc(s_iota, 16)
            for m in range(MC):
                for a in range(PER):
                    r0 = (m * PER + a) * CAP + CAP_L
                    sp.dma_start(yt[a * CAP_C:(a + 1) * CAP_C, m, :], d["ye"][r0:r0 + CAP_C, :]).then_inc(s_t[0], 16)
            for m in range(ML):
                for h in range(2):
                    r0 = (2 * m + h) * CAP
                    sp.dma_start(yt[h * CAP_L:(h + 1) * CAP_L, MC + m, :], d["ye"][r0:r0 + CAP_L, :]).then_inc(s_t[1 + m // 2], 16)
                if m == 0:
                    sp.dma_start(g2b[1][:, :], d["mod"][1:2, G2:G2 + DM].to_broadcast([P, DM])).then_inc(s_g2, 16)
            sp.dma_start(x1[:, :, :], d["x1"].rearrange("(t p) n -> p t n", p=P)).then_inc(s_vec, 16)
            sp.dma_start(g2b[0][:, :], d["mod"][0:1, G2:G2 + DM].to_broadcast([P, DM])).then_inc(s_vec, 16)
            sp.dma_start(lng[:, :], d["ln2_g"].to_broadcast([P, DM])).then_inc(s_vec, 16)
            sp.dma_start(lnb[:, :], d["ln2_b"].to_broadcast([P, DM])).then_inc(s_vec, 16)
            sp.wait_ge(s_vec, 16 * 4)
            for n, t in enumerate(ROWS):
                sp.wait_ge(s_fin, n + 1)
                dst = d["y_sample"][0, t * P:(t + 1) * P, :] if t < CT else d["y_prompt"][0]
                sp.dma_start(dst, x1[:, t, :]).then_inc(s_out, 16)
            sp.wait_ge(s_out, 16 * NT)

        @block.scalar
        def _(act):
            for m in range(MT):
                act.wait_ge(s_t[m // 2], 16 * (MC * PER if m < MC else 4))
                act.activation(yh[:, m, :], yt[:, m, 0:DM], ACT.Copy).then_inc(s_hi, 1)
            for n in range(NT):
                act.wait_ge(s_st, n + 1)
                act.activation(mv[:, 2:3], mv[:, 2:3], ACT.Sqrt).then_inc(s_sd, 1)

        @block.tensor
        def _(pe):
            def add(t, m, first, last_):
                at = t % CT
                for n in range(2):
                    for part in (yh, yl):
                        last = pe.matmul(F[at][:, n * 512:(n + 1) * 512], hot[:, m, at * P:(at + 1) * P], part[:, m, n * 512:(n + 1) * 512],
                                         start=first and part is yh, stop=last_ and part is yl)
                return last

            for m in range(MC):
                pe.wait_ge(s_hot, m + 1)
                last = add(CT, m, m == 0, m == MC - 1)
            last.then_inc(s_mm, 1)
            pe.wait_ge(s_rd, 1)
            for ts in ((0, 1), (2, 3)):
                for m in range(MC, MT):
                    pe.wait_ge(s_hot, m + 1)
                    for t in ts:
                        last = add(t, m, m == MC, m == MT - 1)
                last.then_inc(s_mm, 1)

        @block.gpsimd
        def _(g_):
            g_.wait_ge(s_vec, 16 * 4)
            for n, t in enumerate(ROWS):
                g_.wait_ge(s_nm, n + 1)
                g_.tensor_tensor(x1[:, t, :], x1[:, t, :], lng[:, :], ALU.mult)
                g_.drain()
                g_.tensor_tensor(x1[:, t, :], x1[:, t, :], lnb[:, :], ALU.add).then_inc(s_fin, 1)

        @block.vector
        def _(v):
            def split(m):
                v.wait_ge(s_hi, m + 1)
                c0, c1 = (0, LAT) if m >= MC else (LAT, TOK)
                v.tensor_scalar(hot[:, m, 0:c1 - c0], iota[:, c0:c1], yt[:, m, DM + 1:DM + 2], None, ALU.is_equal)
                v.tensor_tensor(yl[:, m, :], yt[:, m, 0:DM], yh[:, m, :], ALU.subtract).then_inc(s_hot, 1)

            v.wait_ge(s_iota, 16)
            for m in range(MC):
                split(m)
            v.wait_ge(s_g2, 16)
            for n, t in enumerate(ROWS):
                y = mix[n % 2]
                v.drain()
                v.wait_ge(s_mm, (1, 2, 2, 3, 3)[n])
                v.tensor_tensor(y, F[t % CT][:, :], g2b[t // CT][:, :], ALU.mult).then_inc(s_rd, 1)
                if n == 0:
                    for m in range(MC, MT):
                        split(m)
                    v.wait_ge(s_vec, 16 * 4)
                v.drain()
                v.scalar_tensor_tensor(x1[:, t, :], x1[:, t, :], ALPHA, y, ALU.mult, ALU.add)
                v.drain()
                for a in range(2):
                    v.bn_stats(stats[:, a, :], x1[:, t, a * 512:(a + 1) * 512])
                v.drain()
                v.bn_aggr(mv[:, 0:2], stats[:, :, :])
                v.drain()
                v.tensor_scalar(mv[:, 2:3], mv[:, 1:2], LN_EPS, None, ALU.add).then_inc(s_st, 1)
                v.wait_ge(s_sd, n + 1)
                v.reciprocal(mv[:, 3:4], mv[:, 2:3])
                v.drain()
                v.tensor_scalar(x1[:, t, :], x1[:, t, :], mv[:, 0:1], mv[:, 3:4], ALU.subtract, ALU.mult).then_inc(s_nm, 1)


def layer(nc, d):
    sb = lambda ctx, n, s: ctx.enter_context(nc.sbuf_tensor(n, s, F32))
    with ExitStack() as whole:
        ident = sb(whole, "ident_sb", [P, P])
        h_both = sb(whole, "h_both", [P, KD * TOK])
        hT = h_both[:, :].rearrange("p (k t) -> p k t", k=KD)
        h2 = h_both[:, :].rearrange("p (t n) -> p t n", t=NT)
        affT, posT = sb(whole, "affT", [P, NT, NE]), sb(whole, "posT", [P, NT, NE])
        with ExitStack() as mixer:
            x1 = sb(mixer, "x1", [P, NT, DM])
            modulation_phase(nc, d, ident, x1)
            with ExitStack() as lo:
                lora = [sb(lo, f"lora{n}", [P, TOK]) for n in range(3)]
                input_phase(nc, d, ident, x1, hT, lora)
                scan_phase(nc, d, ident, hT, lora, x1[:, :, :].rearrange("p t n -> p (t n)"))
            merge_phase(nc, d, ident, hT, x1, h2, affT, posT)
        expert_phase(nc, d, ident, h2, affT, posT)
        combine_phase(nc, d)


INPUTS = ["x_prompt", "x_sample", "state_fwd", "state_bwd", "c", "c_ctx", "w_ada", "b_ada", "w_in", "conv_w", "w_decay0",
          "w_decay_up", "a0", "a_up", "g_up", "k_k", "k_a", "r_k", "gn_g", "gn_b", "w_fo", "w_ro", "w_out", "ln1_g", "ln1_b",
          "w_router", "w_e1", "w_e3", "w_e2", "ln2_g", "ln2_b"]
OUTPUTS = [("y_prompt", (1, CTX, DM)), ("y_sample", (1, LAT, DM)), ("new_state_fwd", (1, 1, 16, HD, HD)),
           ("new_state_bwd", (1, 1, 16, HD, HD))]


def kernel(**inputs):
    import concourse.bacc as bacc
    from concourse.bass_utils import run_bass_kernel_spmd

    nc = bacc.Bacc("TRN2", target_bir_lowering=False, num_devices=1)
    arrays, d = {}, {}
    for name, a in [(n, inputs[n]) for n in INPUTS] + list(shape_constants().items()):
        a = np.ascontiguousarray(a)
        arrays[f"in_{name}"] = a
        d[name] = nc.dram_tensor(f"in_{name}", a.shape, mybir.dt.from_np(a.dtype), kind="ExternalInput").ap()
    for name, shape in OUTPUTS:
        d[name] = nc.dram_tensor(f"out_{name}", shape, F32, kind="ExternalOutput").ap()
    d["mod"] = nc.dram_tensor("mod_scratch", (2, 6 * DM), F32).ap()
    d["fT"] = nc.dram_tensor("fourierT_scratch", (P, FG, TOK), F32).ap()
    d["yg"] = nc.dram_tensor("ygT_scratch", (P, KD, TOK), F32).ap()
    d["x1"] = nc.dram_tensor("x1_scratch", (TOK, DM), F32).ap()
    d["ye"] = nc.dram_tensor("ye_scratch", (NE * CAP, DM + 2), F32).ap()
    layer(nc, d)
    r = run_bass_kernel_spmd(nc, [arrays], core_ids=[0])
    return tuple(r.results[0][f"out_{name}"] for name, _ in OUTPUTS)
```
